# Optimizing a Trainium2 kernel written in Bass

```python
import jax, jax.numpy as jnp
from jax import lax
import numpy as np

D_MODEL = 1024
BATCH = 1
SEQ = 256
DEPTH = 2

HEAD_DIM = 64
Q_BLOCK = 128
ROPE_THETA = 10000.0
NORM_EPS = 1e-6
NEG_INF = -1e30
N_BRANCHES = 4

FOX_HEADS = 4
FOX_W = FOX_HEADS * HEAD_DIM
FOX_BIAS_CENTER = 3.0
LRU_WIDTH = 256
LRU_BLOCKS = 4
LRU_BW = LRU_WIDTH // LRU_BLOCKS
LRU_CONV = 4
LRU_C = 8.0
DIL_PAIRS = ((128, 1), (512, 4), (2048, 16))
DIL_GROUPS = len(DIL_PAIRS)
DIL_HEADS_PER_GROUP = 2
DIL_HEADS = DIL_GROUPS * DIL_HEADS_PER_GROUP
DIL_W = DIL_HEADS * HEAD_DIM
DIL_OUT_W = DIL_HEADS_PER_GROUP * HEAD_DIM
DIL_KEYS = DIL_PAIRS[0][0] // DIL_PAIRS[0][1] + 1
NSA_HEADS = 4
NSA_KV_HEADS = 1
NSA_W = NSA_HEADS * HEAD_DIM
NSA_KV_W = NSA_KV_HEADS * HEAD_DIM
NSA_CMP_BLOCK = 32
NSA_CMP_STRIDE = 16
NSA_CMP_HIDDEN = 256
NSA_SLC_BLOCK = 64
NSA_TOP_N = 16
NSA_WINDOW = 512
NSA_FORCE_SCORE = 1e6
PEER_HEADS = 8
PEER_N_KEYS = 128
PEER_N_EXPERTS = PEER_N_KEYS * PEER_N_KEYS
PEER_TOPK = 16
PEER_D_KEY = 256
PEER_BLOCK = 128

IN_SPLITS = (FOX_W, FOX_W, FOX_W, FOX_HEADS,
             LRU_WIDTH, LRU_WIDTH,
             DIL_W, DIL_W, DIL_W,
             NSA_W, NSA_KV_W, NSA_KV_W, NSA_KV_W, NSA_KV_W, NSA_KV_W, NSA_KV_W, NSA_HEADS * 3,
             N_BRANCHES * D_MODEL)
IN_WIDTH = sum(IN_SPLITS)

kernel_name = "hybrid_fox_lru_dilated_nsa_peer"

def rms_norm(x, g):
    xf = x.astype(jnp.float32)
    y = xf * lax.rsqrt(jnp.mean(xf * xf, axis=-1, keepdims=True) + NORM_EPS)
    return (y * g.astype(jnp.float32)).astype(x.dtype)

def rope(x, pos):
    half = x.shape[-1] // 2
    freqs = ROPE_THETA ** (-jnp.arange(half, dtype=jnp.float32) / half)
    ang = pos.astype(jnp.float32)[:, None] * freqs[None, :]
    cos = jnp.cos(ang)[None, :, None, :]
    sin = jnp.sin(ang)[None, :, None, :]
    xf = x.astype(jnp.float32)
    x1, x2 = xf[..., :half], xf[..., half:]
    return jnp.concatenate([x1 * cos - x2 * sin, x2 * cos + x1 * sin], axis=-1).astype(x.dtype)

def _unblock(y):
    y = jnp.moveaxis(y, 0, 1)
    return y.reshape((y.shape[0], y.shape[1] * y.shape[2]) + y.shape[3:])

def masked_softmax(logits, mask):
    logits = jnp.where(mask, logits, NEG_INF)
    m = jnp.max(logits, axis=-1, keepdims=True)
    e = jnp.where(mask, jnp.exp(logits - m), 0.0)
    return e / jnp.maximum(jnp.sum(e, axis=-1, keepdims=True), 1e-30)

def fox_attention(q, k, v, f_logit, b_f):
    B, S, H, dh = q.shape
    log_f = jax.nn.log_sigmoid(f_logit.astype(jnp.float32) + b_f.astype(jnp.float32))
    cum = jnp.transpose(jnp.cumsum(log_f, axis=1), (0, 2, 1))
    scale = dh ** -0.5
    k_pos = jnp.arange(S)

    def block(i):
        s0 = i * Q_BLOCK
        qb = lax.dynamic_slice_in_dim(q, s0, Q_BLOCK, axis=1)
        cq = lax.dynamic_slice_in_dim(cum, s0, Q_BLOCK, axis=2)
        logits = jnp.einsum('bqhd,bkhd->bhqk', qb, k).astype(jnp.float32) * scale
        logits = logits + cq[..., None] - cum[:, :, None, :]
        q_pos = s0 + jnp.arange(Q_BLOCK)
        logits = jnp.where(k_pos[None, :] <= q_pos[:, None], logits, NEG_INF)
        p = jax.nn.softmax(logits, axis=-1)
        return jnp.einsum('bhqk,bkhd->bqhd', p.astype(v.dtype), v)

    return _unblock(lax.map(block, jnp.arange(S // Q_BLOCK)))

def rg_lru_branch(x_in, gate, conv_w, conv_b, w_a, b_a, w_x, b_x, lam):
    B, S, C = x_in.shape
    xc = lax.conv_general_dilated(x_in, conv_w[:, None, :], window_strides=(1,),
                                  padding=[(LRU_CONV - 1, 0)],
                                  dimension_numbers=('NWC', 'WIO', 'NWC'),
                                  feature_group_count=C) + conv_b
    xr = xc.reshape(B, S, LRU_BLOCKS, C // LRU_BLOCKS)
    r = jax.nn.sigmoid(jnp.einsum('bsnc,ncd->bsnd', xr, w_a).reshape(B, S, C) + b_a)
    i_g = jax.nn.sigmoid(jnp.einsum('bsnc,ncd->bsnd', xr, w_x).reshape(B, S, C) + b_x)
    log_a = -LRU_C * r.astype(jnp.float32) * jax.nn.softplus(-lam.astype(jnp.float32))
    a = jnp.exp(log_a)
    u = jnp.sqrt(-jnp.expm1(2.0 * log_a)) * (i_g * xc).astype(jnp.float32)

    def combine(left, right):
        a_l, b_l = left
        a_r, b_r = right
        return a_l * a_r, a_r * b_l + b_r

    _, h = lax.associative_scan(combine, (a, u), axis=1)
    return h.astype(x_in.dtype) * jax.nn.gelu(gate)

def dilated_attention(q, k, v):
    B, S, H, dh = q.shape
    G, Hg = DIL_GROUPS, DIL_HEADS_PER_GROUP
    qg = q.reshape(B, S, G, Hg, dh)
    kg = k.reshape(B, S, G, Hg, dh)
    vg = v.reshape(B, S, G, Hg, dh)
    dil = jnp.array([d for _, d in DIL_PAIRS], dtype=jnp.int32)
    steps = jnp.arange(DIL_KEYS)
    g_idx = jnp.arange(G)[:, None, None]
    scale = dh ** -0.5

    def block(i):
        s0 = i * Q_BLOCK
        q_pos = s0 + jnp.arange(Q_BLOCK)
        k_pos = q_pos[None, :, None] - dil[:, None, None] * steps[None, None, :]
        valid = k_pos >= 0
        k_idx = jnp.maximum(k_pos, 0)
        kb = kg[:, k_idx, g_idx]
        vb = vg[:, k_idx, g_idx]
        qb = lax.dynamic_slice_in_dim(qg, s0, Q_BLOCK, axis=1)
        logits = jnp.einsum('bqghd,bgqkhd->bgqhk', qb, kb).astype(jnp.float32) * scale
        logits = jnp.where(valid[None, :, :, None, :], logits, NEG_INF)
        m = jnp.max(logits, axis=-1, keepdims=True)
        e = jnp.exp(logits - m)
        l = jnp.sum(e, axis=-1)
        o = jnp.einsum('bgqhk,bgqkhd->bgqhd', e, vb.astype(jnp.float32)) / l[..., None]
        lse = m[..., 0] + jnp.log(l)
        w = jax.nn.softmax(lse, axis=1)
        return jnp.einsum('bgqh,bgqhd->bqhd', w, o).astype(v.dtype)

    return _unblock(lax.map(block, jnp.arange(S // Q_BLOCK)))

def nsa_attention(q, k_cmp, v_cmp, k_slc, v_slc, k_win, v_win, gate_logits,
                  pe_k, pe_v, w1_k, w2_k, w1_v, w2_v):
    B, S, H, dh = q.shape
    Hkv = k_cmp.shape[2]
    G = H // Hkv
    pos = jnp.arange(S)
    q_rot = rope(q, pos)
    k_slc = rope(k_slc, pos)
    k_win = rope(k_win, pos)
    gates = jax.nn.sigmoid(gate_logits).reshape(B, S, H, 3)
    scale = dh ** -0.5

    n_cmp = (S - NSA_CMP_BLOCK) // NSA_CMP_STRIDE + 1
    cmp_idx = jnp.arange(n_cmp)[:, None] * NSA_CMP_STRIDE + jnp.arange(NSA_CMP_BLOCK)[None, :]

    def compress(kv, pe, w1, w2):
        blocks = kv[:, cmp_idx] + pe[None, None, :, None, :]
        flat = jnp.moveaxis(blocks, 3, 2).reshape(B, n_cmp, Hkv, NSA_CMP_BLOCK * dh)
        return jax.nn.gelu(flat @ w1) @ w2

    kc = compress(k_cmp, pe_k, w1_k, w2_k)
    vc = compress(v_cmp, pe_v, w1_v, w2_v)
    cmp_start = jnp.arange(n_cmp) * NSA_CMP_STRIDE
    cmp_end = cmp_start + NSA_CMP_BLOCK - 1

    n_slc = S // NSA_SLC_BLOCK
    top_n = min(NSA_TOP_N, n_slc)
    slc_start = jnp.arange(n_slc) * NSA_SLC_BLOCK
    overlap = ((cmp_start[:, None] < slc_start[None, :] + NSA_SLC_BLOCK)
               & (cmp_start[:, None] + NSA_CMP_BLOCK > slc_start[None, :])).astype(jnp.float32)
    ks_blocks = jnp.transpose(k_slc.reshape(B, n_slc, NSA_SLC_BLOCK, Hkv, dh), (0, 3, 1, 2, 4))
    vs_blocks = jnp.transpose(v_slc.reshape(B, n_slc, NSA_SLC_BLOCK, Hkv, dh), (0, 3, 1, 2, 4))
    pad = ((0, 0), (NSA_WINDOW, 0), (0, 0), (0, 0))
    k_win_pad = jnp.pad(k_win, pad)
    v_win_pad = jnp.pad(v_win, pad)
    b_idx = jnp.arange(B)[:, None, None, None]
    h_idx = jnp.arange(Hkv)[None, :, None, None]
    blk_ids = jnp.arange(n_slc)

    def block(i):
        s0 = i * Q_BLOCK
        q_pos = s0 + jnp.arange(Q_BLOCK)
        qb = lax.dynamic_slice_in_dim(q, s0, Q_BLOCK, axis=1).reshape(B, Q_BLOCK, Hkv, G, dh)
        qrb = lax.dynamic_slice_in_dim(q_rot, s0, Q_BLOCK, axis=1).reshape(B, Q_BLOCK, Hkv, G, dh)
        lc = jnp.einsum('bqkgd,bckd->bkgqc', qb, kc).astype(jnp.float32) * scale
        p_c = masked_softmax(lc, (cmp_end[None, :] <= q_pos[:, None])[None, None, None])
        o_c = jnp.einsum('bkgqc,bckd->bqkgd', p_c, vc.astype(jnp.float32))
        imp = jnp.einsum('bkgqc,cn->bkqn', p_c, overlap)
        cur = q_pos // NSA_SLC_BLOCK
        forced = ((blk_ids[None, :] == 0) | (blk_ids[None, :] == cur[:, None])
                  | (blk_ids[None, :] == cur[:, None] - 1))
        imp = jnp.where(forced, NSA_FORCE_SCORE, imp)
        imp = jnp.where(blk_ids[None, :] <= cur[:, None], imp, NEG_INF)
        top_val, top_idx = lax.top_k(imp, top_n)
        sel_ok = top_val > 0.5 * NEG_INF
        ksel = ks_blocks[b_idx, h_idx, top_idx]
        vsel = vs_blocks[b_idx, h_idx, top_idx]
        sel_pos = top_idx[..., None] * NSA_SLC_BLOCK + jnp.arange(NSA_SLC_BLOCK)
        sel_mask = sel_ok[..., None] & (sel_pos <= q_pos[None, None, :, None, None])
        n_sel_keys = top_n * NSA_SLC_BLOCK
        ls = jnp.einsum('bqkgd,bkqnld->bkgqnl', qrb, ksel).astype(jnp.float32) * scale
        ls = ls.reshape(B, Hkv, G, Q_BLOCK, n_sel_keys)
        p_s = masked_softmax(ls, sel_mask.reshape(B, Hkv, 1, Q_BLOCK, n_sel_keys))
        o_s = jnp.einsum('bkgqm,bkqmd->bqkgd', p_s,
                         vsel.reshape(B, Hkv, Q_BLOCK, n_sel_keys, dh).astype(jnp.float32))
        kw = lax.dynamic_slice_in_dim(k_win_pad, s0, NSA_WINDOW + Q_BLOCK, axis=1)
        vw = lax.dynamic_slice_in_dim(v_win_pad, s0, NSA_WINDOW + Q_BLOCK, axis=1)
        w_pos = s0 - NSA_WINDOW + jnp.arange(NSA_WINDOW + Q_BLOCK)
        dist = q_pos[:, None] - w_pos[None, :]
        w_mask = (dist >= 0) & (dist < NSA_WINDOW) & (w_pos[None, :] >= 0)
        lw = jnp.einsum('bqkgd,bwkd->bkgqw', qrb, kw).astype(jnp.float32) * scale
        p_w = masked_softmax(lw, w_mask)
        o_w = jnp.einsum('bkgqw,bwkd->bqkgd', p_w, vw.astype(jnp.float32))
        gb = lax.dynamic_slice_in_dim(gates, s0, Q_BLOCK, axis=1).reshape(B, Q_BLOCK, Hkv, G, 3)
        gb = gb.astype(jnp.float32)
        out = gb[..., 0:1] * o_c + gb[..., 1:2] * o_s + gb[..., 2:3] * o_w
        return out.reshape(B, Q_BLOCK, H, dh).astype(q.dtype)

    return _unblock(lax.map(block, jnp.arange(S // Q_BLOCK)))

def peer_ffn(x, w_q, sub_keys, u, v):
    B, S, D = x.shape
    xt = x.reshape(B * S // PEER_BLOCK, PEER_BLOCK, D)
    k = PEER_TOPK

    def block(xb):
        q = (xb @ w_q).reshape(PEER_BLOCK, PEER_HEADS, 2, PEER_D_KEY // 2)
        s = jnp.einsum('thpd,pnd->thpn', q, sub_keys).astype(jnp.float32)
        v_half, i_half = lax.top_k(s, k)
        cand = v_half[:, :, 0, :, None] + v_half[:, :, 1, None, :]
        cand_idx = i_half[:, :, 0, :, None] * PEER_N_KEYS + i_half[:, :, 1, None, :]
        top_s, pos = lax.top_k(cand.reshape(PEER_BLOCK, PEER_HEADS, k * k), k)
        expert = jnp.take_along_axis(cand_idx.reshape(PEER_BLOCK, PEER_HEADS, k * k), pos, axis=-1)
        g = jax.nn.softmax(top_s, axis=-1)
        act = jax.nn.gelu(jnp.einsum('td,thkd->thk', xb, u[expert]))
        return jnp.einsum('thk,thkd->td', (g * act.astype(jnp.float32)).astype(x.dtype), v[expert])

    return lax.map(block, xt).reshape(B, S, D)

def setup_inputs(seed: int = 0) -> dict:
    key = jax.random.key(seed)
    keys = iter(jax.random.split(key, 40))
    L, D = DEPTH, D_MODEL
    f32 = jnp.float32

    def nrm(shape, scale):
        return jax.random.normal(next(keys), shape, f32) * scale

    a_c = jax.random.uniform(next(keys), (L, LRU_WIDTH), f32, 0.9, 0.999)
    a0 = a_c ** (1.0 / LRU_C)
    flat_cmp = NSA_CMP_BLOCK * HEAD_DIM
    return {
        "x": nrm((BATCH, SEQ, D), 1.0),
        "norm1_g": 1.0 + nrm((L, D), 0.02),
        "w_in": nrm((L, D, IN_WIDTH), D ** -0.5),
        "fox_b_f": FOX_BIAS_CENTER + nrm((L, FOX_HEADS), 0.5),
        "lru_conv_w": nrm((L, LRU_CONV, LRU_WIDTH), LRU_CONV ** -0.5),
        "lru_conv_b": nrm((L, LRU_WIDTH), 0.01),
        "lru_w_a": nrm((L, LRU_BLOCKS, LRU_BW, LRU_BW), LRU_BW ** -0.5),
        "lru_b_a": nrm((L, LRU_WIDTH), 0.01),
        "lru_w_x": nrm((L, LRU_BLOCKS, LRU_BW, LRU_BW), LRU_BW ** -0.5),
        "lru_b_x": nrm((L, LRU_WIDTH), 0.01),
        "lru_lambda": jnp.log(a0) - jnp.log1p(-a0),
        "nsa_pe_k": nrm((L, NSA_CMP_BLOCK, HEAD_DIM), 0.02),
        "nsa_pe_v": nrm((L, NSA_CMP_BLOCK, HEAD_DIM), 0.02),
        "nsa_w1_k": nrm((L, flat_cmp, NSA_CMP_HIDDEN), flat_cmp ** -0.5),
        "nsa_w2_k": nrm((L, NSA_CMP_HIDDEN, HEAD_DIM), NSA_CMP_HIDDEN ** -0.5),
        "nsa_w1_v": nrm((L, flat_cmp, NSA_CMP_HIDDEN), flat_cmp ** -0.5),
        "nsa_w2_v": nrm((L, NSA_CMP_HIDDEN, HEAD_DIM), NSA_CMP_HIDDEN ** -0.5),
        "w_br_fox": nrm((L, FOX_W, D), FOX_W ** -0.5),
        "w_br_lru": nrm((L, LRU_WIDTH, D), LRU_WIDTH ** -0.5),
        "w_br_dil": nrm((L, DIL_OUT_W, D), DIL_OUT_W ** -0.5),
        "w_br_nsa": nrm((L, NSA_W, D), NSA_W ** -0.5),
        "w_out": nrm((L, D, D), D ** -0.5),
        "norm2_g": 1.0 + nrm((L, D), 0.02),
        "peer_w_q": nrm((L, D, PEER_HEADS * PEER_D_KEY), D ** -0.5),
        "peer_sub_keys": nrm((L, 2, PEER_N_KEYS, PEER_D_KEY // 2), (PEER_D_KEY // 2) ** -0.5),
        "peer_u": nrm((L, PEER_N_EXPERTS, D), D ** -0.5),
        "peer_v": nrm((L, PEER_N_EXPERTS, D), PEER_HEADS ** -0.5),
        "final_g": 1.0 + nrm((D,), 0.02),
    }

def reference(x, norm1_g, w_in, fox_b_f, lru_conv_w, lru_conv_b, lru_w_a, lru_b_a,
              lru_w_x, lru_b_x, lru_lambda, nsa_pe_k, nsa_pe_v, nsa_w1_k, nsa_w2_k,
              nsa_w1_v, nsa_w2_v, w_br_fox, w_br_lru, w_br_dil, w_br_nsa, w_out,
              norm2_g, peer_w_q, peer_sub_keys, peer_u, peer_v, final_g):
    B, S, D = x.shape
    pos = jnp.arange(S)
    split_points = np.cumsum(IN_SPLITS)[:-1].tolist()

    def heads(t, n):
        return t.reshape(B, S, n, HEAD_DIM)

    for l in range(DEPTH):
        h = rms_norm(x, norm1_g[l])
        proj = h @ w_in[l]
        (fq, fk, fv, ff, lx, lg, dq, dk, dv, nq, nkc, nvc, nks, nvs, nkw, nvw, ng, mg) = \
            jnp.split(proj, split_points, axis=-1)

        o_fox = fox_attention(heads(fq, FOX_HEADS), heads(fk, FOX_HEADS), heads(fv, FOX_HEADS),
                              ff, fox_b_f[l]).reshape(B, S, FOX_W)
        o_lru = rg_lru_branch(lx, lg, lru_conv_w[l], lru_conv_b[l], lru_w_a[l], lru_b_a[l],
                              lru_w_x[l], lru_b_x[l], lru_lambda[l])
        o_dil = dilated_attention(rope(heads(dq, DIL_HEADS), pos), rope(heads(dk, DIL_HEADS), pos),
                                  heads(dv, DIL_HEADS)).reshape(B, S, DIL_OUT_W)
        o_nsa = nsa_attention(heads(nq, NSA_HEADS), heads(nkc, NSA_KV_HEADS), heads(nvc, NSA_KV_HEADS),
                              heads(nks, NSA_KV_HEADS), heads(nvs, NSA_KV_HEADS),
                              heads(nkw, NSA_KV_HEADS), heads(nvw, NSA_KV_HEADS), ng,
                              nsa_pe_k[l], nsa_pe_v[l], nsa_w1_k[l], nsa_w2_k[l],
                              nsa_w1_v[l], nsa_w2_v[l]).reshape(B, S, NSA_W)

        gates = jax.nn.sigmoid(mg).reshape(B, S, N_BRANCHES, D)
        merged = (gates[:, :, 0] * (o_fox @ w_br_fox[l])
                  + gates[:, :, 1] * (o_lru @ w_br_lru[l])
                  + gates[:, :, 2] * (o_dil @ w_br_dil[l])
                  + gates[:, :, 3] * (o_nsa @ w_br_nsa[l]))
        x = x + merged @ w_out[l]

        h2 = rms_norm(x, norm2_g[l])
        x = x + peer_ffn(h2, peer_w_q[l], peer_sub_keys[l], peer_u[l], peer_v[l])

    return rms_norm(x, final_g)


_drawn_inputs = setup_inputs


def setup_inputs(seed=0):
    import zlib

    import numpy as np

    out = dict(_drawn_inputs(seed))
    spreads = {}
    factors = {'lru_b_a': 20.778,
     'lru_b_x': 6.134,
     'nsa_pe_k': 21.395,
     'nsa_pe_v': 3.028,
     'final_g': 9.729}
    for name, (base, spread) in spreads.items():
        noise = np.random.default_rng([zlib.crc32(name.encode()), seed]).standard_normal(out[name].shape)
        drawn = base * np.exp(spread * noise) if base else spread * noise
        out[name] = __import__('jax').numpy.asarray(drawn.astype(out[name].dtype))
    for name, factor in factors.items():
        out[name] = (out[name] * factor).astype(out[name].dtype)
    return out
```

```python
from contextlib import ExitStack

import concourse.bass as bass
from concourse import mybir

ALU = mybir.AluOpType
ACT = mybir.ActivationFunctionType
F32 = mybir.dt.float32
BF16 = mybir.dt.bfloat16
U32 = mybir.dt.uint32
AX = mybir.AxisListType

P = 128
SEQ = 256
NB = SEQ // P
D = 1024
KC = D // P
DEPTH = 2
DH = 64
NEG = -1e30
EPS = 1e-6
FOX_H, DIL_H, NSA_H = 4, 6, 4
N_CMP, CMP_BLOCK, CMP_STRIDE = 15, 32, 16
HEADS = FOX_H + DIL_H + 2 * NSA_H
PH, PK, N_KEYS, TOPK = 8, 2, 128, 16
N_EXPERTS = N_KEYS * N_KEYS
UNITS = NB * PH
RING = 16
NDIAG = 4
WSLOTS = 3
WCOLS = 4096

C_FQ, C_FK, C_FV, C_FF = 0, 256, 512, 768
C_LX, C_LG = 772, 1028
C_DQ, C_DK, C_DV = 1284, 1668, 2052
C_NQ, C_NKC, C_NVC, C_NKS, C_NVS, C_NKW, C_NVW, C_NG = 2436, 2692, 2756, 2820, 2884, 2948, 3012, 3076
SMALL = 3088
SCH = 8
SCW = SMALL // SCH
GCH = 8
GCW = 4 * D // GCH

T_FQ, T_NQ, T_FK, T_LX, T_LG, T_KC, T_VC, T_DQ, T_NQR, T_DK, T_KS, T_KW = 0, 2, 4, 6, 8, 10, 11, 12, 15, 17, 20, 21
T_GROUPS = 22

AUX_ORDER = (["hT0", "hT1", "hT2", "hT3", "params", "subkeys",
              "J0b0", "J0b1", "J1b0", "J1b1", "J2b0", "J2b1", "forget", "ZA", "ZX",
              "J3b0", "J3b1", "J4b0", "J4b1", "J5b0", "J5b1", "J6b0", "J6b1",
              "cmp_hidden", "cmp_kv", "cmp_scores", "cmp_pT", "cmp_out",
              "foxT", "dilT", "nsaT", "mT0", "mT1", "mT2", "mT3", "h2T0", "h2T1", "h2T2", "h2T3"])
AUX = {name: n for n, name in enumerate(AUX_ORDER)}

GELU_C, GELU_S = 0.044715, 0.7978845608028654


def gate_jobs_at(i):
    return [4 + i - i // 3] if i % 3 != 2 else []


def hybrid_decoder(nc, x_in, norm1_g, w_in, fox_b_f, lru_conv_w, lru_conv_b, lru_w_a, lru_b_a,
                   lru_w_x, lru_b_x, lru_lambda, nsa_pe_k, nsa_pe_v, nsa_w1_k, nsa_w2_k,
                   nsa_w1_v, nsa_w2_v, w_br_fox, w_br_lru, w_br_dil, w_br_nsa, w_out,
                   norm2_g, peer_w_q, peer_sub_keys, peer_u, peer_v, final_g,
                   c_ident, c_rope, c_masks, c_cmp, c_pick, out):
    with ExitStack() as ctx:
        def sb(name, shape, dt=F32):
            return ctx.enter_context(nc.sbuf_tensor(name, shape, dt))

        def psum(name, shape):
            return ctx.enter_context(nc.psum_tensor(name, shape, F32))

        sems = []

        def sem(name):
            s = ctx.enter_context(nc.semaphore(name))
            sems.append(s)
            return s

        pmm = psum("pmm", [P, 2, 512])
        psc = psum("psc", [P, 2, 512])
        ppo = psum("ppo", [P, 2, 512])
        paux = psum("paux", [P, 2, 512])

        x = sb("x", [P, NB, D])
        h = sb("h", [P, NB, D])
        hT = sb("hT", [P, KC, SEQ])
        wring = sb("wring", [P, WSLOTS, WCOLS])
        arena = sb("arena", [P, RING * D])
        proj = arena[:, 0:NB * SMALL].rearrange("p (b c) -> p b c", b=NB)
        gate = arena[:, NB * SMALL:NB * (SMALL + 4 * D)].rearrange("p (b c) -> p b c", b=NB)
        rows = arena[:, :].rearrange("p (s d) -> p s d", s=RING)
        TAIL = NB * (SMALL + 4 * D)
        T = sb("T", [P, T_GROUPS, SEQ])
        qT = T[:, 0:PH * PK, :].rearrange("p g t -> p (g t)").rearrange("p (u a t) -> p u a t", u=UNITS, a=PK)
        rope_o = sb("rope_o", [P, NB, 1280])
        gain = rope_o[:, 0, 0:D]
        rope_t = sb("rope_t", [P, 8 * DH])
        merged = rope_o[:, :, 0:D]
        mtmp = rope_t[:, :]
        prob = sb("prob", [P, 2, 384])
        probT = sb("probT", [P, 2, 384])
        probf = prob[:, :, :].rearrange("p a k -> p (a k)")
        probTf = probT[:, :, :].rearrange("p a k -> p (a k)")
        dup = probf[:, 0:512].rearrange("p (b c) -> p b c", b=NB)
        rawp = probTf[0:16, 0:512].rearrange("p (a c) -> p a c", a=2)
        rsub = probTf[:, 512:768].rearrange("p (a c) -> p a c", a=2)
        o_fox = sb("o_fox", [P, NB, 256])
        o_dil = rope_o[:, :, 0:DIL_H * DH].rearrange("p b (h d) -> p b h d", h=DIL_H)
        o_dilm = rope_o[:, :, D:D + P].rearrange("p b (h d) -> p b h d", h=2)
        o_nsa = sb("o_nsa", [P, NB, NSA_H, DH])
        oT = sb("oT", [P, 7, SEQ])
        ident = sb("ident", [P, P])
        ident_b = sb("ident_b", [P, P], BF16)
        masks_f = arena[:, 0:4 * 384]
        masks = sb("masks", [P, 4, 384], BF16)
        rope_c = sb("rope_c", [P, NB, 2, DH])
        cmpm = sb("cmpm", [P, 2, NB, 16])
        pick = sb("pick", [P, 2, 4, P])
        iota16 = sb("iota16", [P, 16])
        nmax = sb("nmax", [P, HEADS, NB])
        lsum = sb("lsum", [P, HEADS, NB])
        rl = sb("rl", [P, HEADS, NB])
        stat = sb("stat", [P, 8])
        eps = sb("eps", [P, 1])
        lp = sb("lp", [P, 2, 8])
        lph = sb("lph", [P, 2, 2])
        peT = sb("peT", [P, 2, 16])
        subT = sb("subT", [P, PK, P])
        wab = sb("wab", [P, 2, 2, P])
        w2kd = sb("w2kd", [P, 2, P])
        w2v = sb("w2v", [P, 2, DH])
        bfb = sb("bfb", [P, FOX_H])
        Y = sb("Y", [P, 6, 10])
        fl = oT[0:4, 5, :]
        cumf = arena[0:4, TAIL + 1760:TAIL + 2016]
        xc, la = (h[:, 0, q * 512:q * 512 + 512].rearrange("p (g t) -> p g t", g=2) for q in range(2))
        lb, ld = (h[:, 1, q * 512:q * 512 + 512].rearrange("p (g t) -> p g t", g=2) for q in range(2))
        le = arena[:, TAIL:TAIL + 512].rearrange("p (g t) -> p g t", g=2)
        csp = sb("csp", [P, 2])
        cin = arena[:, TAIL + 512:TAIL + 992].rearrange("p (t k c) -> p t k c", t=2, k=16)
        hid = sb("hid", [P, 4, 16])
        hg = sb("hg", [P, 3, 4, 16])
        hrep = sb("hrep", [P, 2, 4, 32])
        kcT = sb("kcT", [P, 16])
        vbd = sb("vbd", [P, NSA_H, DH])
        lc = sb("lc", [P, NB, NSA_H, 16])
        pc = sb("pc", [P, NB, NSA_H, 32])
        pcT = arena[:, TAIL + 992:TAIL + 1248]
        oc = arena[:, TAIL + 1248:TAIL + 1760].rearrange("p (b h d) -> p b h d", b=NB, h=NSA_H)
        cst = sb("cst", [P, 4, NB * NSA_H])
        ng = sb("ng", [P, NB, NSA_H, 3])
        dst = sb("dst", [P, 5, NB, DIL_H])
        loff = sb("loff", [P, 1])
        tv = sb("tv", [P, PK, 16])
        ti = sb("ti", [P, PK, 16], U32)
        ga, gin, gt, wv = (oT[:, 6, q * 32:q * 32 + 32].rearrange("p (a k) -> p a k", a=2) for q in range(4))
        gw, actv = (oT[:, 6, q * 16 + 128:q * 16 + 144] for q in range(2))
        diag = T[:, 20:22, :].rearrange("p g (a c) -> p (g a) c", a=2)
        qst = h[:, 0, 0:2 * PK * P].rearrange("p (r a t) -> p r a t", r=2, a=PK)
        tif, cijf, eij = (oT[:, 5, q * 32:q * 32 + 32].rearrange("p (a k) -> p a k", a=2) for q in range(3))
        oTf = oT[:, :, :].rearrange("p g t -> p (g t)")
        srest = oTf[:, 0:256].rearrange("p (a n) -> p a n", a=PK)
        cand = oTf[:, 256:512].rearrange("p (i j) -> p i j", i=16)
        crest = oTf[:, 512:768]
        onehot = oTf[:, 768:1280].rearrange("p (a k j) -> p a k j", a=2, k=16)
        cv = sb("cv", [P, 16])
        cpos = sb("cpos", [P, 16], U32)
        cij = sb("cij", [P, 2, 16], U32)
        eidx = oT[:, 6, 160:192].bitcast(U32).rearrange("p (a k) -> p a k", a=2)
        gidx = sb("gidx", [P, 2, 16], U32)
        sdiff = sb("sdiff", [P, 2, 16])
        sexp = sb("sexp", [P, 2, 16])
        sl = sb("sl", [P, 2, 1])
        srl = sb("srl", [P, 1])
        junk = T[:, 16:20, :].rearrange("p g t -> p (g t)")

        s_const = ctx.enter_context(nc.semaphore("constants_loaded"))
        s_final = ctx.enter_context(nc.semaphore("final_steps"))
        s_out = ctx.enter_context(nc.semaphore("output_ready"))
        s_std = ctx.enter_context(nc.semaphore("final_deviation"))
        s_rec = ctx.enter_context(nc.semaphore("final_reciprocal"))
        s_stored = ctx.enter_context(nc.semaphore("output_stored"))

        row_landed = [ctx.enter_context(nc.semaphore(f"row_landed{i}")) for i in range(RING)]

        w_landed = [sem(f"weights_landed{i}") for i in range(WSLOTS)]
        g_landed = sem("gains_landed")
        p_landed = sem("params_landed")
        ssq_done = sem("squares_summed")
        std_done = sem("deviation_ready")
        h_done = sem("normed_ready")
        pmm_full = sem("pmm_full")
        pmm_dve = sem("pmm_emptied_by_vector")
        pmm_act = sem("pmm_emptied_by_scalar")
        aux_full = sem("aux_full")
        aux_done = sem("aux_emptied")
        dup_done = sem("duplicates_ready")
        rope_done = sem("rotated_ready")
        sp_abs = sem("softplus_input_ready")
        sp_exp = sem("softplus_exp_ready")
        fsp_done = sem("forget_terms_ready")
        cum_done = sem("forget_sums_ready")
        xc_done = sem("lru_conv_ready")
        hb_done = sem("lru_half_bias_ready")
        la_done = sem("lru_log_decay_ready")
        dec_done = sem("lru_decay_ready")
        ysq_done = sem("lru_square_ready")
        root_done = sem("lru_root_ready")
        gin_done = sem("lru_gate_argument_ready")
        gth_done = sem("lru_gate_tanh_ready")
        lru_done = sem("lru_output_ready")
        cin_done = sem("cmp_blocks_ready")
        hgin_done = sem("cmp_gelu_argument_ready")
        hgt_done = sem("cmp_gelu_tanh_ready")
        hrep_done = sem("cmp_hidden_ready")
        lcd_done = sem("cmp_logits_ready")
        lce_done = sem("cmp_exp_ready")
        pc_done = sem("cmp_probs_ready")
        ng_done = sem("nsa_gates_tanh_ready")
        sc_full = sem("scores_full")
        mx_done = sem("max_ready")
        exp_done = sem("probs_ready")
        pt_full = sem("probsT_full")
        pt_done = sem("probsT_ready")
        o_full = sem("head_out_full")
        o_done = sem("head_out_emptied")
        dw_in = sem("dilated_weights_argument")
        dw_exp = sem("dilated_weights_exp")
        od_done = sem("dilated_output_ready")
        m_done = sem("merged_ready")
        es_full = sem("expert_scores_full")
        es_used = sem("expert_scores_used")
        top_done = sem("top_ready")
        sexp_done = sem("expert_softmax_ready")
        gin2_done = sem("expert_gelu_argument_ready")
        gt2_done = sem("expert_gelu_tanh_ready")
        pe_in = sem("expert_block_in_psum")
        pe_back = sem("expert_block_back")
        dots_done = sem("rows_of_u_used")
        sums_done = sem("rows_of_v_used")
        w_ready = sem("expert_weights_ready")
        idx_taken = sem("expert_numbers_taken")
        diag_done = sem("diagonals_ready")
        qst_done = sem("queries_staged")
        dve_step = sem("vector_step")
        pe_half = sem("row_tile_done")
        dve_held = sem("vector_held")
        pool_held = sem("gpsimd_held")
        act_step = sem("scalar_step")

        with nc.Block() as block:
            @block.sync
            def _(sp):
                sp.dma_start(x[:, :, :], x_in[0].rearrange("(b p) d -> p b d", p=P)).then_inc(s_const, 16)
                sp.dma_start(ident[:, :], c_ident).then_inc(s_const, 16)
                sp.dma_start(masks_f[:, :], c_masks).then_inc(s_const, 16)
                sp.dma_start(rope_c[:, :, :, :].rearrange("p b t d -> p (b t d)"), c_rope).then_inc(s_const, 16)
                sp.dma_start(cmpm[:, :, :, :].rearrange("p t b c -> p (t b c)"), c_cmp).then_inc(s_const, 16)
                sp.dma_start(pick[:, :, :, :].rearrange("p s h k -> p (s h k)"), c_pick).then_inc(s_const, 16)
                sp.wait_ge(s_const, 6 * 16)

            @block.gpsimd
            def _(pool):
                nc.gpsimd.memset(wab[:, :, :, :], 0.0)
                nc.gpsimd.memset(vbd[:, :, :], 0.0)
                nc.gpsimd.memset(hrep[:, :, :, :], 0.0)
                nc.gpsimd.memset(pc[:, :, :, :], 0.0)
                nc.gpsimd.memset(loff[:, :], 0.0)
                nc.gpsimd.memset(eps[:, :], EPS)
                nc.gpsimd.iota(iota16[:, :], [[1, 16]], base=0, channel_multiplier=0,
                               allow_small_or_imprecise_dtypes=True)

            @block.vector
            def _(dve):
                dve.wait_ge(s_const, 6 * 16)
                nc.vector.tensor_copy(ident_b[:, :], ident[:, :])
                nc.vector.tensor_copy(masks[:, :, :].rearrange("p m k -> p (m k)"), masks_f[:, :])

        slot = [wring[:, s, :] for s in range(WSLOTS)]

        def w_at(n):
            return slot[n % WSLOTS]

        def w_wait(eng, n):
            eng.wait_ge(w_landed[n % WSLOTS], w_count[n])

        W_SMALL = 0
        W_G01 = SCH
        W_CMP = SCH + 2
        W_G27 = SCH + 4
        W_BR = SCH + 4 + 6
        W_OUT = W_BR + 2
        W_Q = W_OUT + 2
        N_LOADS = W_Q + 4
        parts = [2 if n in (W_BR, W_BR + 1) else 1 for n in range(N_LOADS)]
        w_count = [16 * sum(parts[m] for m in range(n % WSLOTS, n + 1, WSLOTS)) for n in range(N_LOADS)]

        def gate_load(c):
            return W_G01 + c if c < 2 else W_G27 + c - 2

        J_SMALL, J_GATE = 0, 2 * SCH
        J_BR = J_GATE + 2 * GCH
        J_OUT = J_BR + 16
        J_Q = J_OUT + 4

        def pmm_free(eng, j):
            k = j - 2
            if k < 0:
                return
            if k < J_GATE:
                eng.wait_ge(pmm_dve, k + 1)
            elif k < J_BR:
                eng.wait_ge(pmm_act, k - J_GATE + 1)
            elif k < J_Q:
                eng.wait_ge(pmm_dve, J_GATE + k - J_BR + 1)
            else:
                eng.wait_ge(pmm_act, J_BR - J_GATE + k - J_Q + 1)

        def used_up(eng, n):
            if n in (W_CMP, W_CMP + 1):
                eng.wait_ge(aux_full, AUX["cmp_hidden"] + 1)
            elif n < W_G01:
                eng.wait_ge(pmm_full, J_SMALL + 2 * (n - W_SMALL) + 2)
            elif n < W_BR:
                eng.wait_ge(pmm_full, J_GATE + 2 * (n - W_G01 - (2 if n > W_CMP else 0)) + 2)
            elif n < W_OUT:
                eng.wait_ge(pmm_full, J_BR + 8 * (n - W_BR) + 8)
            elif n < W_Q:
                eng.wait_ge(pmm_full, J_OUT + 2 * (n - W_OUT) + 2)
            else:
                eng.wait_ge(pmm_full, J_Q + 2 * (n - W_Q) + 2)

        heads = ([(0, T_FQ + i // 2, i % 2, T_FK + i // 2, i % 2, C_FV + DH * i) for i in range(FOX_H)]
                 + [(1 + i // 2, T_DQ + i // 2, i % 2, T_DK + i // 2, i % 2, C_DV + DH * i) for i in range(DIL_H)]
                 + [(0, T_NQR + i // 2, i % 2, T_KS, i % 2, C_NVS) for i in range(NSA_H)]
                 + [(0, T_NQR + i // 2, i % 2, T_KW, i % 2, C_NVW) for i in range(NSA_H)])
        SLC0, WIN0 = FOX_H + DIL_H, FOX_H + DIL_H + NSA_H

        with nc.Fori(0, DEPTH) as l:
            with nc.Block() as block:

                @block.sync
                def _(sp):
                    sp.dma_start(gain, norm1_g[l].partition_broadcast(P)).then_inc(g_landed, 16)

                    def load(n, dst, src):
                        sp.dma_start(dst, src).then_inc(w_landed[n % WSLOTS], 16)

                    def room(n):
                        if n >= WSLOTS:
                            used_up(sp, n - WSLOTS)

                    def cols(n, w, c0, width):
                        room(n)
                        load(n, w_at(n)[:, 0:KC * width].rearrange("p (k c) -> p k c", k=KC),
                             w[l].rearrange("(k p) c -> p k c", p=P)[:, :, c0:c0 + width])

                    cols(0, w_in, 0, SCW)
                    sp.dma_start(rawp[0:4, 0, :], lru_conv_w[l]).then_inc(p_landed, 16)
                    for r, v in enumerate((lru_conv_b, lru_b_a, lru_b_x, lru_lambda)):
                        sp.dma_start(rawp[4 + r:5 + r, 0, :], v[l].partition_broadcast(1)).then_inc(p_landed, 16)
                    for t, v in enumerate((nsa_pe_k, nsa_pe_v)):
                        sp.dma_start(rawp[:, 1, t * P:(t + 1) * P],
                                     v[l].rearrange("(a b) d -> a (b d)", b=2)).then_inc(p_landed, 16)
                    sp.dma_start(rsub[:, :, :], peer_sub_keys[l].rearrange("a n d -> n a d")).then_inc(p_landed, 16)
                    cols(1, w_in, SCW, SCW)
                    for t, v in enumerate((lru_w_a, lru_w_x)):
                        for half in range(2):
                            sp.dma_start(wab[DH * half:DH * half + DH, t, :, DH * half:DH * half + DH],
                                         v[l].rearrange("(g a) c d -> a c g d", a=2)[half]).then_inc(p_landed, 16)
                    for c in range(2):
                        sp.dma_start(w2kd[:, :, c * DH:(c + 1) * DH],
                                     nsa_w2_k[l].rearrange("(a p) d -> p a d", p=P)).then_inc(p_landed, 16)
                    sp.dma_start(w2v[:, :, :], nsa_w2_v[l].rearrange("(a p) d -> p a d", p=P)).then_inc(p_landed, 16)
                    sp.dma_start(bfb[:, :], fox_b_f[l].partition_broadcast(P)).then_inc(p_landed, 16)
                    for c in range(2, SCH):
                        cols(c, w_in, c * SCW, SCW)
                    for c in range(2):
                        cols(gate_load(c), w_in, SMALL + c * GCW, GCW)
                    for t, v in enumerate((nsa_w1_k, nsa_w1_v)):
                        room(W_CMP + t)
                        load(W_CMP + t, w_at(W_CMP + t).rearrange("p (k c) -> p k c", k=16),
                             v[l].rearrange("(k p) c -> p k c", p=P))
                    for c in range(2, GCH):
                        cols(gate_load(c), w_in, SMALL + c * GCW, GCW)
                    for n, pair in ((W_BR, ((w_br_lru, 2), (w_br_fox, 2))), (W_BR + 1, ((w_br_dil, 1), (w_br_nsa, 2)))):
                        room(n)
                        at = 0
                        for v, k in pair:
                            load(n, w_at(n)[:, at:at + k * D].rearrange("p (k c) -> p k c", k=k),
                                 v[l].rearrange("(k p) c -> p k c", p=P))
                            at += k * D
                    for c in range(2):
                        cols(W_OUT + c, w_out, 512 * c, 512)
                    for c in range(4):
                        cols(W_Q + c, peer_w_q, 512 * c, 512)
                        if c == 0:
                            sp.wait_ge(aux_full, AUX["mT3"] + 1)
                            sp.dma_start(gain, norm2_g[l].partition_broadcast(P)).then_inc(g_landed, 16)

                N_PARAMS = 5 + 2 + 1 + 4 + 2 + 1 + 1

                @block.tensor
                def _(pe):
                    mmul, tp = nc.tensor.matmul, nc.tensor.transpose

                    def aux_bank(name):
                        n = AUX[name]
                        if n >= 2:
                            pe.wait_ge(aux_done, n - 1)
                        return paux[:, n % 2, :]

                    def turn_h(name, src, b, k0):
                        bank = aux_bank(name)
                        for k in range(4):
                            last = tp(bank[:, k * P:(k + 1) * P], src[:, b, (k0 + k) * P:(k0 + k + 1) * P], ident[:, :])
                        last.then_inc(aux_full, 1)

                    def turn_groups(name, parts):
                        bank = aux_bank(name)
                        for k, src in enumerate(parts):
                            last = tp(bank[:, k * P:(k + 1) * P], src, ident[:, :])
                        last.then_inc(aux_full, 1)

                    def project(j, n, b, width):
                        pmm_free(pe, j)
                        w_wait(pe, n)
                        w = w_at(n)[:, 0:KC * width].rearrange("p (k c) -> p k c", k=KC)
                        for k in range(KC):
                            last = mmul(pmm[:, j % 2, 0:width], hT[:, k, b * P:(b + 1) * P], w[:, k, :],
                                        start=(k == 0), stop=(k == KC - 1))
                        last.then_inc(pmm_full, 1)

                    def gate_job(m):
                        project(J_GATE + m, gate_load(m // 2), m % 2, GCW)

                    for b in range(NB):
                        pe.wait_ge(h_done, b + 1)
                        for q in range(2):
                            turn_h(f"hT{2 * b + q}", h, b, 4 * q)
                    pe.wait_ge(p_landed, 16 * N_PARAMS)
                    bank = aux_bank("params")
                    for g in range(2):
                        tp(bank[:, 8 * g:8 * g + 8], rawp[0:8, 0, g * P:(g + 1) * P], ident[0:8, 0:8])
                    for t in range(2):
                        last = tp(bank[:, 16 + 16 * t:32 + 16 * t], rawp[:, 1, t * P:(t + 1) * P], ident[0:16, 0:16])
                    last.then_inc(aux_full, 1)
                    turn_groups("subkeys", [rsub[:, a, :] for a in range(PK)])

                    pe.wait_ge(aux_done, AUX["hT3"] + 1)
                    for c in range(SCH):
                        for b in range(NB):
                            project(J_SMALL + 2 * c + b, W_SMALL + c, b, SCW)

                    pe.wait_ge(pmm_dve, 2 * SCH)
                    for b in range(NB):
                        turn_groups(f"J0b{b}", [proj[:, b, c:c + P] for c in (C_FQ, C_FQ + P, C_NQ, C_NQ + P)])
                    for b in range(NB):
                        turn_groups(f"J1b{b}", [proj[:, b, c:c + P] for c in (C_FK, C_FK + P, C_LX, C_LX + P)])
                    pe.wait_ge(dup_done, 4)
                    for b in range(NB):
                        turn_groups(f"J2b{b}", [proj[:, b, C_LG:C_LG + P], proj[:, b, C_LG + P:C_LG + 2 * P],
                                                dup[:, b, 0:P], dup[:, b, P:2 * P]])
                    gate_job(0)
                    gate_job(1)
                    pe.wait_ge(fsp_done, 1)
                    bank = aux_bank("forget")
                    for b in range(NB):
                        last = tp(bank[0:4, b * P:(b + 1) * P], Y[:, 5, 4 * b:4 * b + 4], ident[:, :])
                    last.then_inc(aux_full, 1)
                    gate_job(2)
                    gate_job(3)
                    pe.wait_ge(xc_done, 1)
                    for t, name in enumerate(("ZA", "ZX")):
                        bank = aux_bank(name)
                        for g in range(2):
                            last = mmul(bank[:, g * SEQ:(g + 1) * SEQ], wab[:, t, g, :], xc[:, g, :], start=True, stop=True)
                        last.then_inc(aux_full, 1)
                    pe.wait_ge(rope_done, NB)
                    for b in range(NB):
                        turn_groups(f"J3b{b}", [rope_o[:, b, c:c + P] for c in (0, P, 2 * P, 768)])
                    for b in range(NB):
                        turn_groups(f"J4b{b}", [rope_o[:, b, 768 + P:768 + 2 * P]])
                    for b in range(NB):
                        turn_groups(f"J5b{b}", [rope_o[:, b, c:c + P] for c in (384, 384 + P, 384 + 2 * P, 1024)])
                    for b in range(NB):
                        turn_groups(f"J6b{b}", [rope_o[:, b, 1152:1280]])
                    pe.wait_ge(cin_done, 1)
                    bank = aux_bank("cmp_hidden")
                    for t in range(2):
                        w_wait(pe, W_CMP + t)
                        w = w_at(W_CMP + t).rearrange("p (k c) -> p k c", k=16)
                        for hh in range(2):
                            o = 16 * (2 * t + hh)
                            for k in range(16):
                                last = mmul(bank[:, o:o + N_CMP], w[:, k, hh * P:(hh + 1) * P], cin[:, t, k, :],
                                            start=(k == 0), stop=(k == 15))
                    last.then_inc(aux_full, 1)

                    def scores(i):
                        m, gq, hq, gk, hk, _ = heads[i]
                        if i >= 2:
                            pe.wait_ge(exp_done, 2 * (i - 1))
                        bank = psc[:, i % 2, 0:384]
                        fox = i < FOX_H
                        mmul(bank, ident_b[:, :], masks[:, m, :], start=True, stop=False, skip_group_check=True)
                        for b in range(NB):
                            o = bank[:, 0:P] if b == 0 else bank[:, P:384]
                            nk = (b + 1) * P
                            last = mmul(o, T[DH * hq:DH * hq + DH, gq, b * P:(b + 1) * P],
                                        T[DH * hk:DH * hk + DH, gk, 0:nk], start=False, stop=not fox,
                                        skip_group_check=True)
                            if fox:
                                mmul(o, cumf[0:4, b * P:(b + 1) * P], E4(1, i, nk), start=False, stop=False,
                                     skip_group_check=True)
                                last = mmul(o, pick[0:4, 0, i, :], cumf[0:4, 0:nk], start=False, stop=True,
                                            skip_group_check=True)
                        last.then_inc(sc_full, 1)

                    def E4(s, i, nk):
                        return pick[0:4, s, i, :] if nk == P else pick[0:4, s, i, :].unsqueeze(1).to_broadcast([4, 2, P])

                    def turn_probs(i):
                        pe.wait_ge(exp_done, 2 * (i + 1))
                        if i >= 1:
                            pe.wait_ge(pt_done, i)
                        for c in range(3):
                            last = tp(ppo[:, 0, c * P:(c + 1) * P], prob[:, i % 2, c * P:(c + 1) * P], ident[:, :])
                        last.then_inc(pt_full, 1)

                    def weighted(i):
                        pe.wait_ge(pt_done, i + 1)
                        if i >= 2:
                            pe.wait_ge(o_done, i - 1)
                        vc = heads[i][5]
                        o = ppo[:, 1, (i % 2) * P:(i % 2) * P + P]
                        mmul(o[:, 0:DH], probT[:, i % 2, 0:P], proj[:, 0, vc:vc + DH], start=True, stop=True)
                        mmul(o[:, DH:P], probT[:, i % 2, P:2 * P], proj[:, 0, vc:vc + DH], start=True, stop=False)
                        mmul(o[:, DH:P], probT[:, i % 2, 2 * P:384], proj[:, 1, vc:vc + DH],
                             start=False, stop=True).then_inc(o_full, 1)

                    pe.wait_ge(cum_done, 1)
                    for i in range(HEADS + 1):
                        if i < HEADS:
                            if i == 0:
                                pe.wait_ge(aux_done, AUX["J6b1"] + 1)
                            scores(i)
                            for m in gate_jobs_at(i):
                                gate_job(m)
                        if i >= 1:
                            weighted(i - 1)
                        if i < HEADS:
                            turn_probs(i)
                        if i == 2:
                            pe.wait_ge(hrep_done, 1)
                            bank = aux_bank("cmp_kv")
                            for hh in range(2):
                                mmul(bank[:, 0:N_CMP], w2kd[:, hh, :], hg[:, 2, hh, 0:N_CMP], start=(hh == 0), stop=(hh == 1))
                            for hh in range(2):
                                last = mmul(bank[:, DH:2 * DH], hrep[:, hh, :, :].rearrange("p a b -> p (a b)"), w2v[:, hh, :],
                                            start=(hh == 0), stop=(hh == 1))
                            last.then_inc(aux_full, 1)
                        if i == 3:
                            pe.wait_ge(aux_done, AUX["cmp_kv"] + 1)
                            bank = aux_bank("cmp_scores")
                            for r in (0, DH):
                                for b in range(NB):
                                    for q in range(r // DH, NSA_H, 2):
                                        o = 16 * (NSA_H * b + q)
                                        last = mmul(bank[:, o:o + N_CMP], T[r:r + DH, T_NQ + q // 2, b * P:(b + 1) * P],
                                                    kcT[r:r + DH, 0:N_CMP], start=True, stop=True)
                                if r == 0:
                                    last.then_inc(pe_half, 1)
                                    pe.wait_ge(pe_half, 1)
                            last.then_inc(aux_full, 1)
                        if i == 6:
                            pe.wait_ge(pc_done, 1)
                            turn_groups("cmp_pT", [pc[:, b, :, :].rearrange("p a c -> p (a c)") for b in range(NB)])
                        if i == 7:
                            pe.wait_ge(aux_done, AUX["cmp_pT"] + 1)
                            bank = aux_bank("cmp_out")
                            for b in range(NB):
                                last = mmul(bank[:, b * SEQ:(b + 1) * SEQ], pcT[:, b * P:(b + 1) * P],
                                            vbd[:, :, :].rearrange("p h d -> p (h d)"), start=True, stop=True)
                            last.then_inc(aux_full, 1)

                    pe.wait_ge(o_done, FOX_H)
                    turn_groups("foxT", [o_fox[:, b, g * P:(g + 1) * P] for g in range(2) for b in range(NB)])

                    def branch(idx, n, off, ks, t0):
                        for b in range(NB):
                            for half in range(2):
                                j = J_BR + 4 * idx + 2 * b + half
                                pmm_free(pe, j)
                                w = w_at(n)[:, off:off + ks * D].rearrange("p (k c) -> p k c", k=ks)
                                for k in range(ks):
                                    last = mmul(pmm[:, j % 2, :], oT[:, t0 + k, b * P:(b + 1) * P],
                                                w[:, k, 512 * half:512 * half + 512], start=(k == 0), stop=(k == ks - 1))
                                last.then_inc(pmm_full, 1)

                    pe.wait_ge(lru_done, 1)
                    w_wait(pe, W_BR)
                    branch(0, W_BR, 0, 2, 0)
                    pe.wait_ge(od_done, 1)
                    turn_groups("dilT", [o_dilm[:, b, :, :].rearrange("p h d -> p (h d)") for b in range(NB)])
                    pe.wait_ge(o_done, HEADS)
                    turn_groups("nsaT", [o_nsa[:, b, 2 * g:2 * g + 2, :].rearrange("p h d -> p (h d)")
                                         for g in range(2) for b in range(NB)])
                    pe.wait_ge(aux_done, AUX["foxT"] + 1)
                    branch(1, W_BR, 2 * D, 2, 2)
                    w_wait(pe, W_BR + 1)
                    pe.wait_ge(aux_done, AUX["dilT"] + 1)
                    branch(2, W_BR + 1, 0, 1, 4)
                    pe.wait_ge(aux_done, AUX["nsaT"] + 1)
                    branch(3, W_BR + 1, D, 2, 5)

                    for b in range(NB):
                        pe.wait_ge(m_done, b + 1)
                        for q in range(2):
                            turn_h(f"mT{2 * b + q}", merged, b, 4 * q)
                    pe.wait_ge(aux_done, AUX["mT3"] + 1)
                    for half in range(2):
                        for b in range(NB):
                            project(J_OUT + 2 * half + b, W_OUT + half, b, 512)

                    for b in range(NB):
                        pe.wait_ge(h_done, NB + b + 1)
                        for q in range(2):
                            turn_h(f"h2T{2 * b + q}", h, b, 4 * q)
                    pe.wait_ge(aux_done, AUX["h2T3"] + 1)

                    def queries(hd):
                        j, n = J_Q + hd, W_Q + hd // 2
                        pmm_free(pe, j)
                        w_wait(pe, n)
                        w = w_at(n).rearrange("p (k c) -> p k c", k=KC)
                        for a in range(PK):
                            c = (hd % 2) * 256 + a * P
                            for k in range(KC):
                                last = mmul(pmm[:, j % 2, a * SEQ:(a + 1) * SEQ], w[:, k, c:c + P], hT[:, k, :],
                                            start=(k == 0), stop=(k == KC - 1))
                        last.then_inc(pmm_full, 1)

                    def key_scores(u, r):
                        pe.wait_ge(qst_done, u + 1)
                        pe.wait_ge(es_used, u + 1)
                        for a in range(PK):
                            last = mmul(psc[:, r, a * P:(a + 1) * P], qst[:, r, a, :], subT[:, a, :],
                                        start=True, stop=True)
                        last.then_inc(es_full, 1)

                    def seed(b):
                        for half in range(2):
                            mmul(paux[:, half, :], ident[:, :], x[:, b, 512 * half:512 * half + 512],
                                 start=True, stop=True)

                    def sums(u):
                        for k in range(TOPK):
                            pe.wait_ge(row_landed[k], (l * UNITS + u) * 32 + 32)
                            pe.wait_ge(diag_done, u * TOPK + k + 1)
                            for half in range(2):
                                last = mmul(paux[:, half, :], diag[:, k % NDIAG, :], rows[:, k, 512 * half:512 * half + 512],
                                            start=False, stop=True, skip_group_check=True)
                            last.then_inc(sums_done, 1)

                    queries(0)
                    queries(1)
                    key_scores(0, 0)
                    key_scores(1, 1)
                    pe.wait_ge(aux_done, AUX["h2T3"] + 1)
                    seed(0)
                    queries(2)
                    queries(3)
                    key_scores(2, 0)
                    key_scores(3, 1)
                    for u in range(2):
                        sums(u)
                        queries(4 + 2 * u)
                        queries(5 + 2 * u)
                        key_scores(u + 4, u)
                    with pe.Fori(1, UNITS // 4) as p:
                        for r in range(2):
                            sums(2 * p + r)
                            key_scores(2 * p + r + 4, r)
                    pe.wait_ge(pe_back, 1)
                    seed(1)
                    with pe.Fori(UNITS // 4, UNITS // 2 - 2) as p:
                        for r in range(2):
                            sums(2 * p + r)
                            key_scores(2 * p + r + 4, r)
                    with pe.Fori(UNITS // 2 - 2, UNITS // 2) as p:
                        for r in range(2):
                            sums(2 * p + r)

                @block.scalar
                def _(act):
                    A = nc.scalar.activation
                    steps = [0]

                    def chain(ins):
                        steps[0] += 1
                        ins.then_inc(act_step, 1)
                        act.wait_ge(act_step, steps[0])

                    def bank_of(name):
                        act.wait_ge(aux_full, AUX[name] + 1)
                        return paux[:, AUX[name] % 2, :]

                    def std(first):
                        for b in range(NB):
                            if not first:
                                act.wait_ge(pmm_dve, J_GATE + 16 + 3 + b)
                            chain(A(h[:, b, :], x[:, b, :], ACT.Square, accum_out=stat[:, b:b + 1]))
                            A(stat[:, 2 + b:3 + b], stat[:, b:b + 1], ACT.Sqrt, bias=eps[:, :], scale=1.0 / D).then_inc(std_done, 1)

                    def take_hT(prefix, scale):
                        for n in range(4):
                            b, q = n // 2, n % 2
                            bank = bank_of(f"{prefix}{n}")
                            A(hT[:, 4 * q:4 * q + 4, b * P:(b + 1) * P], bank.rearrange("p (k t) -> p k t", k=4),
                              ACT.Copy, scale=scale).then_inc(aux_done, 1)

                    def take(name, g0, n, b, scale=1.0):
                        bank = bank_of(name)
                        A(T[:, g0:g0 + n, b * P:(b + 1) * P], bank[:, 0:n * P].rearrange("p (k t) -> p k t", k=n),
                          ACT.Copy, scale=scale).then_inc(aux_done, 1)

                    def gate_tanh(m):
                        c, b = m // 2, m % 2
                        act.wait_ge(pmm_full, J_GATE + m + 1)
                        A(gate[:, b, c * GCW:(c + 1) * GCW], pmm[:, (J_GATE + m) % 2, :], ACT.Tanh,
                          scale=0.5).then_inc(pmm_act, 1)

                    std(True)
                    take_hT("hT", 1.0)
                    bank = bank_of("params")
                    A(lp[:, :, :].rearrange("p g c -> p (g c)"), bank[:, 0:16], ACT.Copy)
                    A(peT[:, :, :].rearrange("p t c -> p (t c)"), bank[:, 16:48], ACT.Copy).then_inc(aux_done, 1)
                    bank = bank_of("subkeys")
                    A(subT[:, :, :].rearrange("p a n -> p (a n)"), bank[:, 0:PK * P], ACT.Copy).then_inc(aux_done, 1)
                    act.wait_ge(pmm_dve, 2 * SCH)
                    for b in range(NB):
                        for t, c in enumerate((C_NKC, C_NVC)):
                            A(dup[:, b, t * P:(t + 1) * P].rearrange("p (a d) -> p a d", a=2),
                              proj[:, b, c:c + DH].unsqueeze(1).to_broadcast([P, 2, DH]), ACT.Copy).then_inc(dup_done, 1)
                    A(ng[:, :, :, :].rearrange("p b h c -> p b (h c)"), proj[:, :, C_NG:C_NG + 12], ACT.Tanh,
                      scale=0.5).then_inc(ng_done, 1)
                    for b in range(NB):
                        take(f"J0b{b}", T_FQ, 4, b, 0.125)
                    for b in range(NB):
                        take(f"J1b{b}", T_FK, 4, b)
                    for b in range(NB):
                        take(f"J2b{b}", T_LG, 4, b)
                    act.wait_ge(sp_abs, 1)
                    A(Y[:, 2, :], Y[:, 1, :], ACT.Exp, scale=-1.0).then_inc(sp_exp, 1)
                    gate_tanh(0)
                    gate_tanh(1)
                    bank = bank_of("forget")
                    A(fl[0:4, :], bank[0:4, 0:SEQ], ACT.Copy).then_inc(aux_done, 1)
                    gate_tanh(2)
                    gate_tanh(3)
                    act.wait_ge(hb_done, 1)
                    for t, (name, dst_) in enumerate((("ZA", lb), ("ZX", ld))):
                        bank = bank_of(name)
                        for g in range(2):
                            last = A(dst_[:, g, :], bank[:, g * SEQ:(g + 1) * SEQ], ACT.Tanh,
                                     bias=lph[:, g, t:t + 1], scale=0.5)
                        last.then_inc(aux_done, 1)
                    for b in range(NB):
                        take(f"J3b{b}", T_DQ, 4, b, 0.125)
                    for b in range(NB):
                        take(f"J4b{b}", T_NQR + 1, 1, b, 0.125)
                    for b in range(NB):
                        take(f"J5b{b}", T_DK, 4, b)
                    for b in range(NB):
                        take(f"J6b{b}", T_KW, 1, b)
                    bank = bank_of("cmp_hidden")
                    A(hid[:, :, 0:N_CMP], bank[:, 0:64].rearrange("p (k c) -> p k c", k=4)[:, :, 0:N_CMP],
                      ACT.Copy).then_inc(aux_done, 1)

                    for i in range(HEADS):
                        act.wait_ge(mx_done, i + 1)
                        if i >= 2:
                            act.wait_ge(pt_full, i - 1)
                        A(prob[:, i % 2, 0:P], psc[:, i % 2, 0:P], ACT.Exp, bias=nmax[:, i, 0:1],
                          accum_out=lsum[:, i, 0:1]).then_inc(exp_done, 1)
                        A(prob[:, i % 2, P:384], psc[:, i % 2, P:384], ACT.Exp, bias=nmax[:, i, 1:2],
                          accum_out=lsum[:, i, 1:2]).then_inc(exp_done, 1)
                        for m in gate_jobs_at(i):
                            gate_tanh(m)
                        if i == 0:
                            act.wait_ge(la_done, 1)
                            A(le[:, :, :], la[:, :, :], ACT.Tanh).then_inc(dec_done, 1)
                            act.wait_ge(dec_done, 1)
                            A(la[:, :, :], la[:, :, :], ACT.Exp).then_inc(dec_done, 1)
                            act.wait_ge(hgin_done, 1)
                            A(hg[:, 1, :, 0:N_CMP], hg[:, 0, :, 0:N_CMP], ACT.Tanh, scale=GELU_S).then_inc(hgt_done, 1)
                        if i == 2:
                            act.wait_ge(ysq_done, 1)
                            A(lb[:, :, :], lb[:, :, :], ACT.Sqrt, scale=0.5).then_inc(root_done, 1)
                            bank = bank_of("cmp_kv")
                            A(kcT[:, 0:N_CMP], bank[:, 0:N_CMP], ACT.Copy, scale=0.5)
                            for q in range(NSA_H):
                                last = A(vbd[32 * q:32 * q + 32, q, :], bank[32 * q:32 * q + 32, DH:2 * DH],
                                         ACT.Copy, scale=0.5)
                            last.then_inc(aux_done, 1)
                        if i == 3:
                            bank = bank_of("cmp_scores")
                            A(lc[:, :, :, 0:N_CMP], bank[:, 0:P].rearrange("p (b h c) -> p b h c", b=NB, h=NSA_H)[:, :, :, 0:N_CMP],
                              ACT.Copy).then_inc(aux_done, 1)
                            act.wait_ge(gin_done, 1)
                            A(ld[:, :, :], le[:, :, :], ACT.Tanh, scale=GELU_S).then_inc(gth_done, 1)
                        if i == 5:
                            act.wait_ge(lcd_done, 1)
                            A(lc[:, :, :, 0:N_CMP], lc[:, :, :, 0:N_CMP], ACT.Exp).then_inc(lce_done, 1)
                        if i == 6:
                            bank = bank_of("cmp_pT")
                            A(pcT[:, :], bank[:, 0:SEQ], ACT.Copy).then_inc(aux_done, 1)
                        if i == 7:
                            bank = bank_of("cmp_out")
                            A(oc[:, :, :, :].rearrange("p b h d -> p (b h d)"), bank, ACT.Copy).then_inc(aux_done, 1)
                        if i == 12:
                            act.wait_ge(dw_in, 1)
                            A(dst[:, 1, :, :], dst[:, 0, :, :], ACT.Exp).then_inc(dw_exp, 1)

                    bank = bank_of("foxT")
                    A(oT[:, 2:4, :].rearrange("p g t -> p (g t)"), bank, ACT.Copy).then_inc(aux_done, 1)
                    bank = bank_of("dilT")
                    A(oT[:, 4, :], bank[:, 0:SEQ], ACT.Copy).then_inc(aux_done, 1)
                    bank = bank_of("nsaT")
                    A(oT[:, 5:7, :].rearrange("p g t -> p (g t)"), bank, ACT.Copy).then_inc(aux_done, 1)
                    take_hT("mT", 0.5)
                    std(False)
                    take_hT("h2T", 1.0)

                    def take_q(hd):
                        j = J_Q + hd
                        act.wait_ge(pmm_full, j + 1)
                        for a in range(PK):
                            last = A(qT[:, hd::PH, a, :], pmm[:, j % 2, a * SEQ:(a + 1) * SEQ].rearrange("p (b t) -> p b t", b=NB),
                                     ACT.Copy)
                        last.then_inc(pmm_act, 1)

                    def stage(u, r, first=False):
                        if not first:
                            act.wait_ge(es_full, u - 1)
                        A(qst[:, r, :, :], qT[:, u, :, :], ACT.Copy).then_inc(qst_done, 1)

                    def softmax_exp(u, r):
                        act.wait_ge(top_done, u + 1)
                        A(sexp[:, r, :], sdiff[:, r, :], ACT.Exp, accum_out=sl[:, r, :]).then_inc(sexp_done, 1)

                    def gelu_tanh(u, r):
                        act.wait_ge(gin2_done, u + 1)
                        A(gt[:, r, :], gin[:, r, :], ACT.Tanh, scale=GELU_S).then_inc(gt2_done, 1)

                    def diagonals(u, r):
                        act.wait_ge(w_ready, u + 1)
                        for k in range(TOPK):
                            act.wait_ge(sums_done, u * TOPK + k + 1 + RING - NDIAG)
                            A(diag[:, k % NDIAG, :], ident[:, :], ACT.Copy, scale=wv[:, r, k:k + 1]).then_inc(diag_done, 1)

                    def into_psum(b):
                        A(ppo[:, :, :].rearrange("p a c -> p (a c)"), h[:, b, :], ACT.Copy).then_inc(pe_in, 1)
                        act.wait_ge(pe_in, b + 1)

                    def back(b):
                        act.wait_ge(sums_done, (b + 1) * PH * TOPK + RING)
                        A(x[:, b, :], paux[:, :, :].rearrange("p a c -> p (a c)"), ACT.Copy).then_inc(pe_back, 1)

                    act.wait_ge(aux_done, AUX["h2T3"] + 1)
                    into_psum(0)
                    take_q(0)
                    take_q(1)
                    act.wait_ge(pmm_act, 2 * GCH + 2)
                    stage(0, 0, True)
                    stage(1, 1, True)
                    softmax_exp(0, 0)
                    softmax_exp(1, 1)
                    take_q(2)
                    take_q(3)
                    act.wait_ge(pmm_act, 2 * GCH + 4)
                    stage(2, 0)
                    stage(3, 1)
                    for u in range(2):
                        gelu_tanh(u, u)
                        diagonals(u, u)
                        take_q(4 + 2 * u)
                        take_q(5 + 2 * u)
                        act.wait_ge(pmm_act, 2 * GCH + 6 + 2 * u)
                        stage(u + 4, u)
                        softmax_exp(u + 2, u)

                    def unit(u, r):
                        gelu_tanh(u, r)
                        diagonals(u, r)
                        stage(u + 4, r)
                        softmax_exp(u + 2, r)

                    with act.Fori(1, UNITS // 4 - 1) as p:
                        unit(2 * p, 0)
                        unit(2 * p + 1, 1)
                    unit(PH - 2, 0)
                    gelu_tanh(PH - 1, 1)
                    act.wait_ge(dots_done, PH * TOPK)
                    into_psum(1)
                    diagonals(PH - 1, 1)
                    stage(PH + 3, 1)
                    softmax_exp(PH + 1, 1)
                    back(0)
                    with act.Fori(UNITS // 4, UNITS // 2 - 2) as p:
                        unit(2 * p, 0)
                        unit(2 * p + 1, 1)
                    for u in range(UNITS - 4, UNITS):
                        gelu_tanh(u, u % 2)
                        diagonals(u, u % 2)
                        if u + 2 < UNITS:
                            softmax_exp(u + 2, u % 2)
                    back(1)

                @block.gpsimd
                def _(pool):
                    pool.wait_ge(pmm_dve, J_GATE + 16)

                    def gather(p, r):
                        pool.wait_ge(top_done, 2 * p + r + 1)
                        pool.sem_inc(pool_held, 1)
                        nc.gpsimd.tensor_copy(gidx[:, r, :], eidx[:, r, :]).then_inc(idx_taken, 1)
                        pool.wait_ge(idx_taken, 2 * p + r + 1)
                        for t, table in enumerate((peer_u, peer_v)):
                            for k in range(TOPK):
                                pool.wait_ge((sums_done, dots_done)[t], (2 * p + r) * TOPK + k + 1)
                                pool.sem_inc(pool_held, 1)
                                nc.gpsimd.indirect_dma_start(
                                    out=rows[:, k, :], out_offset=None,
                                    in_=table.rearrange("l e d -> (l e) d"),
                                    in_offset=bass.IndirectOffsetOnAxis(ap=gidx[:, r, k:k + 1], axis=0),
                                ).then_inc(row_landed[k], 16)

                    with pool.Fori(0, UNITS // 2) as p:
                        gather(p, 0)
                        gather(p, 1)

                @block.vector
                def _(dve):
                    V = nc.vector
                    steps = [0]
                    TT, TS, STT = V.tensor_tensor, V.tensor_scalar, V.scalar_tensor_tensor

                    def chain(ins):
                        steps[0] += 1
                        ins.then_inc(dve_step, 1)
                        dve.wait_ge(dve_step, steps[0])

                    def norm(n0, g_count):
                        dve.wait_ge(g_landed, 16 * g_count)
                        for b in range(NB):
                            dve.wait_ge(std_done, n0 + b + 1)
                            chain(V.reciprocal(stat[:, 4 + b:5 + b], stat[:, 2 + b:3 + b]))
                            STT(h[:, b, :], x[:, b, :], stat[:, 4 + b:5 + b], gain, ALU.mult,
                                ALU.mult).then_inc(h_done, 1)

                    norm(0, 1)

                    def rope_part(b, src, n, dst):
                        s = proj[:, b, src:src + n * DH].rearrange("p (n t d) -> p n t d", n=n, t=2)
                        t = rope_t[:, 0:n * DH].rearrange("p (n t d) -> p n t d", n=n, t=2)
                        o = dst.rearrange("p (n t d) -> p n t d", n=n, t=2)
                        sn = rope_c[:, b, 1, :].rearrange("p (t d) -> p t d", t=2)
                        TT(t[:, :, 0, :], s[:, :, 1, :], sn[:, 0, :].unsqueeze(1).to_broadcast([P, n, 32]), ALU.mult)
                        TT(t[:, :, 1, :], s[:, :, 0, :], sn[:, 1, :].unsqueeze(1).to_broadcast([P, n, 32]), ALU.mult)
                        chain(TT(o.rearrange("p n t d -> p n (t d)"), s.rearrange("p n t d -> p n (t d)"),
                                 rope_c[:, b, 0, :].unsqueeze(1).to_broadcast([P, n, DH]), ALU.mult))
                        of, tf = o.rearrange("p n t d -> p (n t d)"), t.rearrange("p n t d -> p (n t d)")
                        chain(TT(of, of, tf, ALU.add))

                    for c in range(SCH):
                        for b in range(NB):
                            j = 2 * c + b
                            dve.wait_ge(pmm_full, j + 1)
                            V.tensor_copy(proj[:, b, c * SCW:(c + 1) * SCW], pmm[:, j % 2, 0:SCW]).then_inc(pmm_dve, 1)
                        if c == 5:
                            dve.wait_ge(pmm_dve, 12)
                            for b in range(NB):
                                rope_part(b, C_DQ, DIL_H, rope_o[:, b, 0:384])
                                rope_part(b, C_DK, DIL_H, rope_o[:, b, 384:768])
                        if c == 1:
                            dve.wait_ge(p_landed, 16 * N_PARAMS)
                            dve.wait_ge(pmm_dve, 4)
                            dve.wait_ge(aux_done, AUX["params"] + 1)
                            y = Y[:, 0, :]
                            TT(y[:, 0:8].rearrange("p (b h) -> p b h", b=NB), proj[:, :, C_FF:C_FF + 4],
                               bfb[:, :].unsqueeze(1).to_broadcast([P, NB, 4]), ALU.add)
                            chain(V.tensor_copy(y[:, 8:10], lp[:, :, 7]))
                            chain(TS(Y[:, 3, :], y, -1.0, None, ALU.mult))
                            TT(Y[:, 1, :], y, Y[:, 3, :], ALU.max).then_inc(sp_abs, 1)
                            TS(Y[:, 5, :], Y[:, 3, :], 0.0, None, ALU.max)
                            TS(lph[:, :, :], lp[:, :, 5:7], 0.5, None, ALU.mult).then_inc(hb_done, 1)
                    dve.wait_ge(pmm_dve, 2 * SCH)
                    dve.wait_ge(sp_exp, 1)
                    e, z, z2, acc = Y[:, 2, :], Y[:, 3, :], Y[:, 4, :], Y[:, 1, :]
                    chain(TS(z, e, 2.0, None, ALU.add))
                    chain(V.reciprocal(z, z))
                    chain(TT(z, z, e, ALU.mult))
                    chain(TT(z2, z, z, ALU.mult))
                    chain(TS(acc, z2, 1.0 / 17, None, ALU.mult))
                    for n in (15, 13, 11, 9, 7, 5, 3):
                        chain(STT(acc, acc, 1.0 / n, z2, ALU.add, ALU.mult))
                    chain(STT(acc, acc, 1.0, z, ALU.add, ALU.mult))
                    STT(Y[:, 5, :], acc, 2.0, Y[:, 5, :], ALU.mult, ALU.add).then_inc(fsp_done, 1)
                    dve.wait_ge(fsp_done, 1)
                    chain(TS(csp[:, :], Y[:, 5, 8:10], -4.0, None, ALU.mult))
                    dve.wait_ge(aux_done, AUX["J1b1"] + 1)
                    for g in range(2):
                        chain(TS(xc[:, g, :], T[:, T_LX + g, :], lp[:, g, 3:4], lp[:, g, 4:5], ALU.mult, ALU.add))
                        for s in range(1, 4):
                            last = STT(xc[:, g, s:SEQ], T[:, T_LX + g, 0:SEQ - s], lp[:, g, 3 - s:4 - s], xc[:, g, s:SEQ],
                                       ALU.mult, ALU.add)
                            if (g, s) != (1, 3):
                                chain(last)
                    last.then_inc(xc_done, 1)
                    dve.wait_ge(xc_done, 1)
                    dve.wait_ge(aux_done, AUX["J2b1"] + 1)
                    for t in range(2):
                        for half in range(2):
                            r = slice(DH * half, DH * half + DH)
                            src = T[r, T_KC + t, :].rearrange("p (c s u) -> p s u c", s=8, u=2)
                            for q in range(2):
                                last = TT(cin[r, t, 8 * q:8 * q + 8, :], src[:, :, half, q:q + N_CMP],
                                          peT[r, t, 8 * q:8 * q + 8].unsqueeze(2).to_broadcast([DH, 8, N_CMP]), ALU.add)
                    last.then_inc(cin_done, 1)
                    for b in range(NB):
                        rope_part(b, C_NQ, NSA_H, rope_o[:, b, 768:1024])
                        for t, c in enumerate((C_NKS, C_NKW)):
                            o = rope_o[:, b, 1024 + t * P:1024 + (t + 1) * P]
                            rope_part(b, c, 1, o[:, 0:DH])
                            last = V.tensor_copy(o[:, DH:P], o[:, 0:DH])
                            if t == 0:
                                chain(last)
                        last.then_inc(rope_done, 1)
                    dve.wait_ge(rope_done, 2)
                    ones4 = oT[0:4, 6, :]
                    chain(V.memset(ones4, 1.0))
                    dve.wait_ge(aux_done, AUX["forget"] + 1)
                    V.tensor_tensor_scan(cumf[0:4, :], ones4, fl[0:4, :], 0.0, ALU.mult, ALU.add).then_inc(cum_done, 1)
                    dve.wait_ge(cum_done, 1)
                    dve.wait_ge(aux_done, AUX["ZX"] + 1)
                    for g in range(2):
                        last = TS(la[:, g, :], lb[:, g, :], 1.0, csp[:, g:g + 1], ALU.add, ALU.mult)
                    last.then_inc(la_done, 1)
                    dve.wait_ge(aux_done, AUX["cmp_hidden"] + 1)
                    hv = hid[:, :, 0:N_CMP]
                    chain(TT(hg[:, 1, :, 0:N_CMP], hv, hv, ALU.mult))
                    chain(TS(hg[:, 1, :, 0:N_CMP], hg[:, 1, :, 0:N_CMP], GELU_C, 1.0, ALU.mult, ALU.add))
                    TT(hg[:, 0, :, 0:N_CMP], hg[:, 1, :, 0:N_CMP], hv, ALU.mult).then_inc(hgin_done, 1)

                    def head_max(i):
                        dve.wait_ge(sc_full, i + 1)
                        V.tensor_reduce(nmax[:, i, 0:1], psc[:, i % 2, 0:P], AX.X, ALU.max, negate=True)
                        V.tensor_reduce(nmax[:, i, 1:2], psc[:, i % 2, P:384], AX.X, ALU.max, negate=True).then_inc(mx_done, 1)

                    def take_probsT(i):
                        dve.wait_ge(pt_full, i + 1)
                        if i >= 2:
                            dve.wait_ge(o_full, i - 1)
                        V.tensor_copy(probT[:, i % 2, :], ppo[:, 0, 0:384]).then_inc(pt_done, 1)

                    def take_out(i):
                        dve.wait_ge(o_full, i + 1)
                        o = ppo[:, 1, (i % 2) * P:(i % 2) * P + P].rearrange("p (b d) -> p b d", b=NB)
                        if FOX_H <= i < SLC0:
                            V.tensor_copy(o_dil[:, :, i - FOX_H, :], o).then_inc(o_done, 1)
                            return
                        dve.wait_ge(exp_done, 2 * (i + 1))
                        chain(V.reciprocal(rl[:, i, :], lsum[:, i, :]))
                        if i < FOX_H:
                            for b in range(NB):
                                last = TS(o_fox[:, b, i * DH:(i + 1) * DH], o[:, b, :], rl[:, i, b:b + 1], None, ALU.mult)
                        else:
                            q = (i - SLC0) % NSA_H
                            chain(TT(rl[:, i, :], rl[:, i, :], ng[:, :, q, 1 if i < WIN0 else 2], ALU.mult))
                            for b in range(NB):
                                last = STT(o_nsa[:, b, q, :], o[:, b, :], rl[:, i, b:b + 1], o_nsa[:, b, q, :],
                                           ALU.mult, ALU.add)
                        last.then_inc(o_done, 1)
                        dve.wait_ge(o_done, i + 1)

                    def lru_root():
                        dve.wait_ge(dec_done, 1)
                        chain(TS(lb[:, :, :], le[:, :, :], -1.0, None, ALU.add))
                        chain(V.reciprocal(lb[:, :, :], lb[:, :, :]))
                        TT(lb[:, :, :], lb[:, :, :], le[:, :, :], ALU.mult).then_inc(ysq_done, 1)
                        dve.wait_ge(ysq_done, 1)
                        chain(STT(xc[:, :, :], ld[:, :, :], 1.0, xc[:, :, :], ALU.add, ALU.mult))
                        lg = T[:, T_LG:T_LG + 2, :]
                        chain(TT(le[:, :, :], lg, lg, ALU.mult))
                        chain(TS(le[:, :, :], le[:, :, :], GELU_C, 1.0, ALU.mult, ALU.add))
                        TT(le[:, :, :], le[:, :, :], lg, ALU.mult).then_inc(gin_done, 1)

                    def lru_scan():
                        dve.wait_ge(root_done, 1)
                        chain(TT(xc[:, :, :], xc[:, :, :], lb[:, :, :], ALU.mult))
                        dve.wait_ge(dec_done, 2)
                        for g in range(2):
                            last = V.tensor_tensor_scan(lb[:, g, :], la[:, g, :], xc[:, g, :], 0.0, ALU.mult, ALU.add)
                        chain(last)

                    def lru_out():
                        dve.wait_ge(gth_done, 1)
                        lg = T[:, T_LG:T_LG + 2, :]
                        chain(STT(ld[:, :, :], ld[:, :, :], 1.0, lg, ALU.add, ALU.mult))
                        STT(oT[:, 0:2, :], lb[:, :, :], 0.5, ld[:, :, :], ALU.mult, ALU.mult).then_inc(lru_done, 1)

                    def cmp_hidden():
                        dve.wait_ge(hgt_done, 1)
                        chain(STT(hg[:, 2, :, 0:N_CMP], hg[:, 1, :, 0:N_CMP], 1.0, hid[:, :, 0:N_CMP], ALU.add, ALU.mult))
                        V.tensor_copy(hrep[:, :, :, 0:N_CMP],
                                      hg[:, 2, 2:4, 0:N_CMP].unsqueeze(2).to_broadcast([P, 2, NSA_H, N_CMP])).then_inc(hrep_done, 1)

                    def cmp_softmax_in():
                        dve.wait_ge(aux_done, AUX["cmp_scores"] + 1)
                        v = lc[:, :, :, 0:N_CMP]
                        chain(TT(v, v, cmpm[:, 0, :, 0:N_CMP].unsqueeze(2).to_broadcast([P, NB, NSA_H, N_CMP]), ALU.add))
                        m8 = cst[:, 0, :].rearrange("p (b h) -> p b h", b=NB)
                        chain(V.tensor_reduce(m8, v, AX.X, ALU.max))
                        TT(v, v, m8.unsqueeze(3).to_broadcast([P, NB, NSA_H, N_CMP]), ALU.subtract).then_inc(lcd_done, 1)

                    def cmp_softmax_out():
                        dve.wait_ge(lce_done, 1)
                        v = pc[:, :, :, 0:N_CMP]
                        TT(v, lc[:, :, :, 0:N_CMP], cmpm[:, 1, :, 0:N_CMP].unsqueeze(2).to_broadcast([P, NB, NSA_H, N_CMP]),
                           ALU.mult).then_inc(pc_done, 1)
                        dve.wait_ge(pc_done, 1)
                        m8 = cst[:, 1, :].rearrange("p (b h) -> p b h", b=NB)
                        chain(V.tensor_reduce(m8, v, AX.X, ALU.add))
                        chain(TS(cst[:, 1, :], cst[:, 1, :], 1e-30, None, ALU.max))
                        chain(V.reciprocal(cst[:, 1, :], cst[:, 1, :]))
                        dve.wait_ge(ng_done, 1)
                        chain(TS(ng[:, :, :, :], ng[:, :, :, :], 1.0, 0.5, ALU.add, ALU.mult))
                        chain(TT(m8, m8, ng[:, :, :, 0], ALU.mult))

                    def cmp_out():
                        dve.wait_ge(aux_done, AUX["cmp_out"] + 1)
                        chain(TT(o_nsa[:, :, :, :].rearrange("p b h d -> p (b h) d"), oc[:, :, :, :].rearrange("p b h d -> p (b h) d"),
                                 cst[:, 1, :].unsqueeze(2).to_broadcast([P, NB * NSA_H, DH]), ALU.mult))

                    dn = nmax[:, FOX_H:SLC0, :].rearrange("p (g s) b -> p b g s", s=2)
                    dl = lsum[:, FOX_H:SLC0, :].rearrange("p (g s) b -> p b g s", s=2)

                    def d5(k):
                        return dst[:, k, :, :].rearrange("p b (g s) -> p b g s", s=2)

                    def dil_in():
                        m = cst[:, 2, 0:4].rearrange("p (b s) -> p b s", b=NB)
                        chain(TT(m, dn[:, :, 0, :], dn[:, :, 1, :], ALU.min))
                        chain(TT(m, m, dn[:, :, 2, :], ALU.min))
                        for g in range(3):
                            last = TT(d5(0)[:, :, g, :], m, dn[:, :, g, :], ALU.subtract)
                        last.then_inc(dw_in, 1)

                    def dil_out():
                        dve.wait_ge(dw_exp, 1)
                        w = d5(1)
                        for g in range(3):
                            last = TT(d5(2)[:, :, g, :], w[:, :, g, :], dl[:, :, g, :], ALU.mult)
                        chain(last)
                        s = cst[:, 3, 0:4].rearrange("p (b s) -> p b s", b=NB)
                        chain(TT(s, d5(2)[:, :, 0, :], d5(2)[:, :, 1, :], ALU.add))
                        chain(TT(s, s, d5(2)[:, :, 2, :], ALU.add))
                        chain(V.reciprocal(s, s))
                        for g in range(3):
                            last = TT(d5(3)[:, :, g, :], w[:, :, g, :], s, ALU.mult)
                        chain(last)
                        ov = o_dil[:, :, :, :]
                        for b in range(NB):
                            last = TT(ov[:, b, :, :], ov[:, b, :, :], dst[:, 3, b, :].unsqueeze(2).to_broadcast([P, DIL_H, DH]), ALU.mult)
                        chain(last)
                        chain(TT(o_dilm[:, :, :, :], ov[:, :, 0:2, :], ov[:, :, 2:4, :], ALU.add))
                        TT(o_dilm[:, :, :, :], o_dilm[:, :, :, :], ov[:, :, 4:6, :], ALU.add).then_inc(od_done, 1)

                    for i in range(HEADS + 1):
                        if i < HEADS:
                            head_max(i)
                        if i >= 1:
                            take_out(i - 1)
                        if i < HEADS:
                            take_probsT(i)
                        if i == 0:
                            lru_root()
                        if i == 1:
                            cmp_hidden()
                        if i == 3:
                            lru_scan()
                        if i == 4:
                            lru_out()
                            cmp_softmax_in()
                        if i == 5:
                            cmp_softmax_out()
                        if i == 8:
                            cmp_out()
                        if i == 11:
                            dil_in()
                        if i == 13:
                            dil_out()

                    jd = J_GATE
                    for idx, g in enumerate((1, 0, 2, 3)):
                        for b in range(NB):
                            for half in range(2):
                                j = J_BR + 4 * idx + 2 * b + half
                                dve.wait_ge(pmm_full, j + 1)
                                dve.wait_ge(pmm_act, 2 * GCH)
                                m = merged[:, b, 512 * half:512 * half + 512]
                                tgt = m if idx == 0 else mtmp
                                STT(tgt, gate[:, b, g * D + 512 * half:g * D + 512 * half + 512], 1.0, pmm[:, j % 2, :],
                                    ALU.add, ALU.mult).then_inc(pmm_dve, 1)
                                jd += 1
                                dve.wait_ge(pmm_dve, jd)
                                if idx:
                                    last = TT(m, m, mtmp, ALU.add)
                                    if idx == 3 and half == 1:
                                        last.then_inc(m_done, 1)
                                        dve.wait_ge(m_done, b + 1)
                                    else:
                                        chain(last)
                    for half in range(2):
                        for b in range(NB):
                            j = J_OUT + 2 * half + b
                            dve.wait_ge(pmm_full, j + 1)
                            xs = x[:, b, 512 * half:512 * half + 512]
                            TT(xs, pmm[:, j % 2, :], xs, ALU.add).then_inc(pmm_dve, 1)
                            jd += 1
                    dve.wait_ge(pmm_dve, jd)
                    norm(NB, 2)

                    V.sem_inc(sums_done, RING)
                    V.sem_inc(es_used, 2)

                    LINKS_SUM = 5
                    count = [steps[0], 0]

                    def link(ins):
                        count[1] += 1
                        ins.then_inc(dve_step, 1)
                        dve.wait_ge(dve_step, count[0] + count[1])

                    def held():
                        dve.sem_inc(dve_held, 1)

                    def top(u, r, u_prev=None):
                        dve.wait_ge(es_full, u + 1)
                        s = [psc[:, r, a * P:(a + 1) * P] for a in range(PK)]
                        pairs = range(PK)

                        def both(f):
                            f(0)
                            return f(1)
                        held()
                        link(both(lambda a: V.max(tv[:, a, 0:8], s[a])))
                        held()
                        both(lambda a: V.max_index(ti[:, a, 0:8], tv[:, a, 0:8], s[a]))
                        last = both(lambda a: V.match_replace(srest[:, a, :], tv[:, a, 0:8], s[a], -3.0e38))
                        last.then_inc(es_used, 1)
                        dve.wait_ge(es_used, u + 3)
                        held()
                        link(both(lambda a: V.max(tv[:, a, 8:16], srest[:, a, :])))
                        held()
                        link(both(lambda a: V.max_index(ti[:, a, 8:16], tv[:, a, 8:16], srest[:, a, :])))
                        TS(tif[:, 0, :], ti[:, 0, :], float(N_KEYS), loff[:, 0:1], ALU.mult, ALU.add)
                        V.tensor_copy(tif[:, 1, :], ti[:, 1, :])
                        link(TT(cand[:, :, :], tv[:, 0, :].unsqueeze(2).to_broadcast([P, 16, 16]),
                                tv[:, 1, :].unsqueeze(1).to_broadcast([P, 16, 16]), ALU.add))
                        cf = cand[:, :, :].rearrange("p i j -> p (i j)")
                        held()
                        link(V.max(cv[:, 0:8], cf))
                        held()
                        V.max_index(cpos[:, 0:8], cv[:, 0:8], cf)
                        link(V.match_replace(crest[:, :], cv[:, 0:8], cf, -3.0e38))
                        held()
                        link(V.max(cv[:, 8:16], crest[:, :]))
                        held()
                        link(V.max_index(cpos[:, 8:16], cv[:, 8:16], crest[:, :]))
                        TS(cij[:, 0, :], cpos[:, :], 4, None, ALU.logical_shift_right)
                        link(TS(cij[:, 1, :], cpos[:, :], 15, None, ALU.bitwise_and))
                        link(V.tensor_copy(cijf[:, :, :], cij[:, :, :]))
                        f3 = onehot[:, :, :, :].rearrange("p a k j -> p (a k) j")
                        link(TT(f3, cijf[:, :, :].rearrange("p a k -> p (a k)").unsqueeze(2).to_broadcast([P, 32, 16]),
                                iota16[:, :].unsqueeze(1).to_broadcast([P, 32, 16]), ALU.is_equal))
                        link(TT(onehot[:, :, :, :], onehot[:, :, :, :], tif[:, :, :].unsqueeze(2).to_broadcast([P, 2, 16, 16]), ALU.mult))
                        link(V.tensor_reduce(eij[:, :, :].rearrange("p a k -> p (a k)"), f3, AX.X, ALU.add))
                        TS(sdiff[:, r, :], cv[:, :], cv[:, 0:1], None, ALU.subtract)
                        if u_prev is not None:
                            dve.wait_ge(idx_taken, u_prev + 1)
                        TT(eidx[:, r, :], eij[:, 0, :], eij[:, 1, :], ALU.add).then_inc(top_done, 1)

                    def dots(u, r):
                        h_ps = ppo[:, :, :].rearrange("p a c -> p (a c)")
                        for k in range(TOPK):
                            dve.wait_ge(row_landed[k], (l * UNITS + u) * 32 + 16)
                            V.tensor_tensor_reduce(out=junk[:, :], in0=rows[:, k, :], in1=h_ps, scale=1.0, scalar=0.0,
                                                   op0=ALU.mult, op1=ALU.add,
                                                   accum_out=actv[:, k:k + 1]).then_inc(dots_done, 1)
                            dve.wait_ge(dots_done, u * TOPK + k + 1)
                        link(TT(ga[:, 0, :], actv[:, :], actv[:, :], ALU.mult))
                        link(TS(ga[:, 1, :], ga[:, 0, :], GELU_C, 1.0, ALU.mult, ALU.add))
                        TT(gin[:, r, :], ga[:, 1, :], actv[:, :], ALU.mult).then_inc(gin2_done, 1)
                        dve.wait_ge(sexp_done, u + 1)
                        link(V.reciprocal(srl[:, :], sl[:, r, :]))
                        link(TS(gw[:, :], sexp[:, r, :], srl[:, 0:1], 0.5, ALU.mult, ALU.mult))
                        dve.wait_ge(gt2_done, u + 1)
                        link(STT(ga[:, 0, :], gt[:, r, :], 1.0, actv[:, :], ALU.add, ALU.mult))
                        TT(wv[:, r, :], ga[:, 0, :], gw[:, :], ALU.mult).then_inc(w_ready, 1)

                    top(0, 0)
                    links_top = count[1]
                    top(1, 1)
                    start, links_pair = count[0] + count[1], 2 * (links_top + LINKS_SUM)

                    def pair(p, more):
                        count[0], count[1] = p * links_pair + start, 0
                        for r in range(2):
                            dots(2 * p + r, r)
                            if more:
                                top(2 * p + r + 2, r, 2 * p + r)
                        assert not more or count[1] == links_pair

                    dve.wait_ge(pe_in, 1)
                    with dve.Fori(0, UNITS // 4) as p:
                        pair(p, True)
                    dve.wait_ge(pe_in, 2)
                    with dve.Fori(UNITS // 4, UNITS // 2 - 1) as p:
                        pair(p, True)
                    pair(UNITS // 2 - 1, False)
                    TS(loff[:, :], loff[:, :], float(N_EXPERTS), None, ALU.add)

            numbers = [s.num for s in sems]
            assert numbers == list(range(numbers[0], numbers[-1] + 1))
            nc.sync.sem_clear(range(numbers[0], numbers[-1] + 1))
            nc.all_engine_barrier()

        with nc.Block() as block:
            @block.sync
            def _(sp):
                sp.dma_start(gain, final_g.partition_broadcast(P)).then_inc(s_final, 16)
                for b in range(NB):
                    sp.wait_ge(s_out, 1 + b)
                    sp.dma_start(out[0].rearrange("(b p) d -> p b d", p=P)[:, b, :], h[:, b, :]).then_inc(s_stored, 16)
                sp.wait_ge(s_stored, 16 * NB)

            @block.scalar
            def _(act):
                for b in range(NB):
                    nc.scalar.activation(junk[:, :], x[:, b, :], ACT.Square, accum_out=stat[:, b:b + 1]).then_inc(s_std, 1)
                    act.wait_ge(s_std, 2 * b + 1)
                    nc.scalar.activation(stat[:, 2 + b:3 + b], stat[:, b:b + 1], ACT.Sqrt, bias=eps[:, :],
                                         scale=1.0 / D).then_inc(s_std, 1)

            @block.vector
            def _(dve):
                dve.wait_ge(s_final, 16)
                for b in range(NB):
                    dve.wait_ge(s_std, 2 * b + 2)
                    nc.vector.reciprocal(stat[:, 4 + b:5 + b], stat[:, 2 + b:3 + b]).then_inc(s_rec, 1)
                    dve.wait_ge(s_rec, b + 1)
                    nc.vector.scalar_tensor_tensor(h[:, b, :], x[:, b, :], stat[:, 4 + b:5 + b], gain,
                                                   ALU.mult, ALU.mult).then_inc(s_out, 1)


_INS = ['x', 'norm1_g', 'w_in', 'fox_b_f', 'lru_conv_w', 'lru_conv_b', 'lru_w_a', 'lru_b_a',
        'lru_w_x', 'lru_b_x', 'lru_lambda', 'nsa_pe_k', 'nsa_pe_v', 'nsa_w1_k', 'nsa_w2_k',
        'nsa_w1_v', 'nsa_w2_v', 'w_br_fox', 'w_br_lru', 'w_br_dil', 'w_br_nsa', 'w_out',
        'norm2_g', 'peer_w_q', 'peer_sub_keys', 'peer_u', 'peer_v', 'final_g']


def _constants(np):
    f = np.float32
    pos = np.arange(256, dtype=f)
    freqs = (f(10000.0) ** (-np.arange(32, dtype=f) / f(32))).astype(f)
    ang = (pos[:, None] * freqs[None, :]).astype(f)
    cos, sin = np.cos(ang).astype(f), np.sin(ang).astype(f)
    rope = np.stack([np.concatenate([cos, cos], 1), np.concatenate([-sin, sin], 1)], 1)
    rope = rope.reshape(2, 128, 2, 64).transpose(1, 0, 2, 3).reshape(128, 256)
    q = np.arange(128)
    masks = np.zeros((128, 4, 384), f)
    for b in range(2):
        dist = (b * 128 + q)[:, None] - np.arange((b + 1) * 128)[None, :]
        ok = [dist >= 0, (dist >= 0) & (dist <= 128), (dist >= 0) & (dist % 4 == 0), (dist >= 0) & (dist % 16 == 0)]
        for m in range(4):
            masks[:, m, 128 * b:128 * b + (b + 1) * 128] = np.where(ok[m], 0.0, NEG)
    end = 16 * np.arange(16) + 31
    ok = end[None, None, :] <= (np.arange(2)[None, :, None] * 128 + q[:, None, None])
    cmp = np.stack([np.where(ok, 0.0, NEG), np.where(ok, 1.0, 0.0)], 1).astype(f)
    pick = np.zeros((128, 2, 4, 128), f)
    for h in range(4):
        pick[h, 0, h] = 1.0
        pick[h, 1, h] = -1.0
    return {"c_ident": np.eye(128, dtype=f), "c_rope": np.ascontiguousarray(rope),
            "c_masks": masks.reshape(128, -1), "c_cmp": cmp.reshape(128, -1), "c_pick": pick.reshape(128, -1)}


def kernel(**inputs):
    import numpy as _np
    import concourse.bacc as _bacc
    from concourse import mybir as _mybir
    from concourse.bass_utils import run_bass_kernel_spmd as _run

    nc = _bacc.Bacc("TRN2", target_bir_lowering=False, num_devices=1)
    arrays, args = {}, []
    for name, a in [(n, inputs[n]) for n in _INS] + list(_constants(_np).items()):
        a = _np.ascontiguousarray(a)
        arrays[f"in_{name}_dram"] = a
        args.append(nc.dram_tensor(f"in_{name}_dram", a.shape, _mybir.dt.from_np(a.dtype), kind="ExternalInput").ap())
    args.append(nc.dram_tensor("out_0_dram", (1, SEQ, D), _mybir.dt.float32, kind="ExternalOutput").ap())
    hybrid_decoder(nc, *args)
    r = _run(nc, [arrays], core_ids=[0])
    return r.results[0]["out_0_dram"]
```

```python
from contextlib import ExitStack

import concourse.bass as bass
from concourse import mybir

ALU = mybir.AluOpType
ACT = mybir.ActivationFunctionType
F32 = mybir.dt.float32
BF16 = mybir.dt.bfloat16
U32 = mybir.dt.uint32
AX = mybir.AxisListType

P = 128
SEQ = 256
CMP_HID = 256
NB = SEQ // P
D = 1024
KC = D // P
DEPTH = 2
DH = 64
NEG = -1e30
EPS = 1e-6
FOX_H, DIL_H, NSA_H = 4, 6, 4
N_CMP, CMP_BLOCK, CMP_STRIDE = 15, 32, 16
HEADS = FOX_H + DIL_H + 2 * NSA_H
PH, PK, N_KEYS, TOPK = 8, 2, 128, 16
N_EXPERTS = N_KEYS * N_KEYS
UNITS = NB * PH
RING = 16
NDIAG = 4
WSLOTS = 3
WCOLS = 4096

C_FQ, C_FK, C_FV, C_FF = 0, 256, 512, 768
C_LX, C_LG = 772, 1028
C_DQ, C_DK, C_DV = 1284, 1668, 2052
C_NQ, C_NKC, C_NVC, C_NKS, C_NVS, C_NKW, C_NVW, C_NG = 2436, 2692, 2756, 2820, 2884, 2948, 3012, 3076
SMALL = 3088
SCH = 8
SCW = SMALL // SCH
GCH = 8
GCW = 4 * D // GCH

T_FQ, T_NQ, T_FK, T_LX, T_LG, T_KC, T_VC, T_DQ, T_NQR, T_DK, T_KS, T_KW = 0, 2, 4, 6, 8, 10, 11, 12, 15, 17, 20, 21
T_GROUPS = 22

AUX_ORDER = (["hT0", "hT1", "hT2", "hT3", "params", "subkeys",
              "J0b0", "J0b1", "J1b0", "J1b1", "J2b0", "J2b1", "forget", "ZA", "ZX",
              "J3b0", "J3b1", "J4b0", "J4b1", "J5b0", "J5b1", "J6b0", "J6b1",
              "cmp_raw", "cmp_hidden", "cmp_kv", "cmp_scores", "cmp_pT", "cmp_out",
              "foxT", "dilT", "nsaT", "mT0", "mT1", "mT2", "mT3", "h2T0", "h2T1", "h2T2", "h2T3"])
AUX = {name: n for n, name in enumerate(AUX_ORDER)}

GELU_C, GELU_S = 0.044715, 0.7978845608028654


def gate_jobs_at(i):
    return [4 + i - i // 3] if i % 3 != 2 else []


def hybrid_decoder(nc, x_in, gains, w_in, fox_b_f, lru_conv_w, lru_conv_b, lru_w_a, lru_b_a,
                   lru_w_x, lru_b_x, lru_lambda, nsa_pe_k, nsa_pe_v, nsa_w1_k, nsa_w2_k,
                   nsa_w1_v, nsa_w2_v, w_br_fox, w_br_lru, w_br_dil, w_br_nsa, w_out,
                   norm2_g, peer_w_q, peer_sub_keys, peer_u, peer_v,
                   c_ident, c_rope, c_masks, c_cmp, c_pick, out):
    with ExitStack() as ctx:
        def sb(name, shape, dt=F32):
            return ctx.enter_context(nc.sbuf_tensor(name, shape, dt))

        def psum(name, shape):
            return ctx.enter_context(nc.psum_tensor(name, shape, F32))

        sems = []

        def sem(name):
            s = ctx.enter_context(nc.semaphore(name))
            sems.append(s)
            return s

        pmm = psum("pmm", [P, 2, 512])
        psc = psum("psc", [P, 2, 512])
        ppo = psum("ppo", [P, 2, 512])
        paux = psum("paux", [P, 2, 512])

        x = sb("x", [P, NB, D])
        h = sb("h", [P, NB, D])
        hT = sb("hT", [P, KC, SEQ])
        wring = sb("wring", [P, WSLOTS, WCOLS])
        arena = sb("arena", [P, RING * D])
        proj = arena[:, 0:NB * SMALL].rearrange("p (b c) -> p b c", b=NB)
        gate = arena[:, NB * SMALL:NB * (SMALL + 4 * D)].rearrange("p (b c) -> p b c", b=NB)
        rows = arena[:, :].rearrange("p (s d) -> p s d", s=RING)
        TAIL = NB * (SMALL + 4 * D)
        T = sb("T", [P, T_GROUPS, SEQ])
        qT = T[:, 0:PH * PK, :].rearrange("p g t -> p (g t)").rearrange("p (u a t) -> p u a t", u=UNITS, a=PK)
        w_out_at = [arena[:, 0:KC * 512].rearrange("p (k c) -> p k c", k=KC),
                    T[:, 4:20, :].rearrange("p g t -> p (g t)").rearrange("p (k c) -> p k c", k=KC)]
        rope_o = sb("rope_o", [P, NB, 1280])
        gain = rope_o[:, 0, 0:D]
        rope_t = sb("rope_t", [P, 8 * DH])
        merged = rope_o[:, :, 0:D]
        mtmp = rope_t[:, :]
        prob = sb("prob", [P, 2, 384])
        probT = sb("probT", [P, 2, 384])
        probf = prob[:, :, :].rearrange("p a k -> p (a k)")
        probTf = probT[:, :, :].rearrange("p a k -> p (a k)")
        dup = probf[:, 0:512].rearrange("p (b c) -> p b c", b=NB)
        rawp = probTf[0:16, 0:512].rearrange("p (a c) -> p a c", a=2)
        rsub = probTf[:, 512:768].rearrange("p (a c) -> p a c", a=2)
        o_fox = sb("o_fox", [P, NB, 256])
        o_dil = rope_o[:, :, 0:DIL_H * DH].rearrange("p b (h d) -> p b h d", h=DIL_H)
        o_dilm = rope_o[:, :, D:D + P].rearrange("p b (h d) -> p b h d", h=2)
        o_nsa = sb("o_nsa", [P, NB, NSA_H, DH])
        oT = sb("oT", [P, 7, SEQ])
        w_q3_at = ([[rope_o[:, 1, 512 * q + 256 * e:512 * q + 256 * e + 256] for e in range(2)] for q in range(2)]
                   + [[t[:, 256 * e:256 * e + 256] for e in range(2)]
                      for t in (probf, probTf, rope_t, o_fox[:, :, :].rearrange("p b c -> p (b c)"),
                                o_nsa[:, :, :, :].rearrange("p b h d -> p (b h d)"))]
                   + [[rope_o[:, e, D:D + 256] for e in range(2)]])
        ident = sb("ident", [P, P])
        ident_b = sb("ident_b", [P, P], BF16)
        masks_f = arena[:, 0:4 * 384]
        masks = sb("masks", [P, 4, 384], BF16)
        rope_c = sb("rope_c", [P, NB, 2, DH])
        cmpm = sb("cmpm", [P, 2, NB, 16])
        pick = sb("pick", [P, 2, 4, P])
        iota16 = sb("iota16", [P, 16])
        nmax = sb("nmax", [P, HEADS, NB])
        lsum = sb("lsum", [P, HEADS, NB])
        rl = sb("rl", [P, HEADS, NB])
        stat = sb("stat", [P, 8])
        eps = sb("eps", [P, 1])
        lp = sb("lp", [P, 2, 8])
        lph = sb("lph", [P, 2, 2])
        peT = sb("peT", [P, 2, 16])
        subT = sb("subT", [P, PK, P])
        wab = sb("wab", [P, 2, 2, P])
        w2kd = sb("w2kd", [P, 2, P])
        w2v = sb("w2v", [P, 2, DH])
        bfb = sb("bfb", [P, FOX_H])
        Y = sb("Y", [P, 6, 10])
        fl = oT[0:4, 5, :]
        cumf = arena[0:4, TAIL + 1760:TAIL + 2016]
        xc, la = (h[:, 0, q * 512:q * 512 + 512].rearrange("p (g t) -> p g t", g=2) for q in range(2))
        lb, ld = (h[:, 1, q * 512:q * 512 + 512].rearrange("p (g t) -> p g t", g=2) for q in range(2))
        le = arena[:, TAIL:TAIL + 512].rearrange("p (g t) -> p g t", g=2)
        csp = sb("csp", [P, 2])
        cin = arena[:, TAIL + 512:TAIL + 992].rearrange("p (t k c) -> p t k c", t=2, k=16)
        hid = sb("hid", [P, 4, 16])
        hid_raw = oT[0:N_CMP, 0:2, :].rearrange("p g t -> p (g t)")
        hg = sb("hg", [P, 3, 4, 16])
        hrep = sb("hrep", [P, 2, 4, 32])
        kcT = sb("kcT", [P, 16])
        vbd = sb("vbd", [P, NSA_H, DH])
        lc = sb("lc", [P, NB, NSA_H, 16])
        pc = sb("pc", [P, NB, NSA_H, 32])
        pcT = arena[:, TAIL + 992:TAIL + 1248]
        oc = arena[:, TAIL + 1248:TAIL + 1760].rearrange("p (b h d) -> p b h d", b=NB, h=NSA_H)
        cst = sb("cst", [P, 4, NB * NSA_H])
        ng = sb("ng", [P, NB, NSA_H, 3])
        dst = sb("dst", [P, 5, NB, DIL_H])
        loff = sb("loff", [P, 1])
        tv = sb("tv", [P, PK, 16])
        ti = sb("ti", [P, PK, 16], U32)
        ga, gin, gt, wv = (oT[:, 6, q * 32:q * 32 + 32].rearrange("p (a k) -> p a k", a=2) for q in range(4))
        gw, actv = (oT[:, 6, q * 16 + 128:q * 16 + 144] for q in range(2))
        diag = T[:, 20:22, :].rearrange("p g (a c) -> p (g a) c", a=2)
        qst = h[:, 0, 0:2 * PK * P].rearrange("p (r a t) -> p r a t", r=2, a=PK)
        tif, cijf, eij = (oT[:, 5, q * 32:q * 32 + 32].rearrange("p (a k) -> p a k", a=2) for q in range(3))
        oTf = oT[:, :, :].rearrange("p g t -> p (g t)")
        srest = oTf[:, 0:256].rearrange("p (a n) -> p a n", a=PK)
        cand = oTf[:, 256:512].rearrange("p (i j) -> p i j", i=16)
        crest = oTf[:, 512:768]
        onehot = oTf[:, 768:1280].rearrange("p (a k j) -> p a k j", a=2, k=16)
        cv = sb("cv", [P, 16])
        cpos = sb("cpos", [P, 16], U32)
        cij = sb("cij", [P, 2, 16], U32)
        eidx = oT[:, 6, 160:192].bitcast(U32).rearrange("p (a k) -> p a k", a=2)
        gidx = sb("gidx", [P, 2, 16], U32)
        sdiff = sb("sdiff", [P, 2, 16])
        sexp = sb("sexp", [P, 2, 16])
        sl = sb("sl", [P, 2, 1])
        srl = sb("srl", [P, 1])
        junk = T[:, 16:20, :].rearrange("p g t -> p (g t)")

        s_masks = ctx.enter_context(nc.semaphore("masks_loaded"))
        s_const = ctx.enter_context(nc.semaphore("constants_loaded"))
        s_out = ctx.enter_context(nc.semaphore("output_ready"))
        s_std = ctx.enter_context(nc.semaphore("final_deviation"))
        s_rec = ctx.enter_context(nc.semaphore("final_reciprocal"))
        s_stored = ctx.enter_context(nc.semaphore("output_stored"))

        row_landed = [ctx.enter_context(nc.semaphore(f"row_landed{i}")) for i in range(RING)]

        wo_landed = [sem(f"output_weights_landed{i}") for i in range(2)]
        wq3_landed = sem("last_query_weights_landed")
        w_landed = [sem(f"weights_landed{i}") for i in range(WSLOTS)]
        g_landed = sem("gains_landed")
        p_landed = sem("params_landed")
        ssq_done = sem("squares_summed")
        std_done = sem("deviation_ready")
        h_done = sem("normed_ready")
        pmm_full = sem("pmm_full")
        pmm_dve = sem("pmm_emptied_by_vector")
        pmm_act = sem("pmm_emptied_by_scalar")
        aux_full = sem("aux_full")
        aux_done = sem("aux_emptied")
        dup_done = sem("duplicates_ready")
        rope_done = sem("rotated_ready")
        sp_abs = sem("softplus_input_ready")
        sp_exp = sem("softplus_exp_ready")
        fsp_done = sem("forget_terms_ready")
        cum_done = sem("forget_sums_ready")
        xc_done = sem("lru_conv_ready")
        hb_done = sem("lru_half_bias_ready")
        la_done = sem("lru_log_decay_ready")
        dec_done = sem("lru_decay_ready")
        ysq_done = sem("lru_square_ready")
        root_done = sem("lru_root_ready")
        gin_done = sem("lru_gate_argument_ready")
        gth_done = sem("lru_gate_tanh_ready")
        lru_done = sem("lru_output_ready")
        cin_done = sem("cmp_blocks_ready")
        hgin_done = sem("cmp_gelu_argument_ready")
        hgt_done = sem("cmp_gelu_tanh_ready")
        hrep_done = sem("cmp_hidden_ready")
        lcd_done = sem("cmp_logits_ready")
        lce_done = sem("cmp_exp_ready")
        pc_done = sem("cmp_probs_ready")
        ng_done = sem("nsa_gates_tanh_ready")
        sc_full = sem("scores_full")
        mx_done = sem("max_ready")
        exp_done = sem("probs_ready")
        pt_full = sem("probsT_full")
        pt_done = sem("probsT_ready")
        o_full = sem("head_out_full")
        o_done = sem("head_out_emptied")
        dw_in = sem("dilated_weights_argument")
        dw_exp = sem("dilated_weights_exp")
        od_done = sem("dilated_output_ready")
        m_done = sem("merged_ready")
        es_full = sem("expert_scores_full")
        es_used = sem("expert_scores_used")
        top_done = sem("top_ready")
        sexp_done = sem("expert_softmax_ready")
        gin2_done = sem("expert_gelu_argument_ready")
        gt2_done = sem("expert_gelu_tanh_ready")
        pe_in = sem("expert_block_in_psum")
        pe_back = sem("expert_block_back")
        dots_done = sem("rows_of_u_used")
        sums_done = sem("rows_of_v_used")
        w_ready = sem("expert_weights_ready")
        idx_taken = sem("expert_numbers_taken")
        diag_done = sem("diagonals_ready")
        qst_done = sem("queries_staged")
        dve_step = sem("vector_step")
        pe_half = sem("row_tile_done")
        dve_held = sem("vector_held")
        pool_held = sem("gpsimd_held")
        act_step = sem("scalar_step")

        with nc.Block() as block:
            @block.sync
            def _(sp):
                sp.dma_start(masks_f[:, :], c_masks).then_inc(s_masks, 16)
                sp.dma_start(ident[:, :], c_ident).then_inc(s_masks, 16)
                sp.dma_start(rope_c[:, :, :, :].rearrange("p b t d -> p (b t d)"), c_rope).then_inc(s_const, 16)
                sp.dma_start(cmpm[:, :, :, :].rearrange("p t b c -> p (t b c)"), c_cmp).then_inc(s_const, 16)
                sp.dma_start(pick[0:4, :, :, :].rearrange("p s h k -> p (s h k)"), c_pick).then_inc(s_const, 16)
                sp.dma_start(gain, gains[0].partition_broadcast(P)).then_inc(s_const, 16)
                sp.dma_start(x[:, :, :], x_in[0].rearrange("(b p) d -> p b d", p=P)).then_inc(s_const, 16)

            @block.gpsimd
            def _(pool):
                nc.gpsimd.memset(wab[:, :, :, :], 0.0)
                nc.gpsimd.memset(vbd[:, :, :], 0.0)
                nc.gpsimd.memset(hrep[:, :, :, :], 0.0)
                nc.gpsimd.memset(pc[:, :, :, :], 0.0)
                nc.gpsimd.memset(loff[:, :], 0.0)
                nc.gpsimd.memset(eps[:, :], EPS)
                nc.gpsimd.iota(iota16[:, :], [[1, 16]], base=0, channel_multiplier=0,
                               allow_small_or_imprecise_dtypes=True)

            @block.vector
            def _(dve):
                dve.wait_ge(s_masks, 2 * 16)
                nc.vector.tensor_copy(ident_b[:, :], ident[:, :])
                nc.vector.tensor_copy(masks[:, :, :].rearrange("p m k -> p (m k)"), masks_f[:, :])

        slot = [wring[:, s, :] for s in range(WSLOTS)]

        def w_at(n):
            return slot[n % WSLOTS]

        def w_wait(eng, n):
            eng.wait_ge(w_landed[n % WSLOTS], w_count[n])

        W_SMALL = 0
        W_G01 = SCH
        W_CMP = SCH + 2
        W_G27 = SCH + 4
        W_BR = SCH + 4 + 6
        W_Q = W_BR + 2
        N_LOADS = W_Q + 3
        parts = [2 if n in (W_BR, W_BR + 1) else 1 for n in range(N_LOADS)]
        w_count = [16 * sum(parts[m] for m in range(n % WSLOTS, n + 1, WSLOTS)) for n in range(N_LOADS)]

        def gate_load(c):
            return W_G01 + c if c < 2 else W_G27 + c - 2

        J_SMALL, J_GATE = 0, 2 * SCH
        J_BR = J_GATE + 2 * GCH
        J_OUT = J_BR + 16
        J_Q = J_OUT + 4
        J_Q00 = J_OUT + 2
        J_OUTS = (J_OUT, J_OUT + 1, J_OUT + 3, J_OUT + 4)

        PE_SHARE = 11

        BR_ORDER = ((0, 0), (1, 0), (2, 0), (0, 1), (3, 0), (1, 1), (2, 1), (3, 1))

        def pmm_free(eng, j):
            k = j - 2
            if k < 0:
                return
            if k < J_GATE:
                eng.wait_ge(pmm_dve, k + 1)
            elif k < J_BR:
                eng.wait_ge(pmm_act, k - J_GATE + 1)
            elif k < J_Q00:
                eng.wait_ge(pmm_dve, J_GATE + k - J_BR + 1)
            elif k == J_Q00:
                eng.wait_ge(pmm_act, J_BR - J_GATE + 1)
            elif k <= J_OUTS[3]:
                eng.wait_ge(pmm_dve, J_GATE + k - J_BR)
            else:
                eng.wait_ge(pmm_act, J_BR - J_GATE + k - J_Q + 1)

        def used_up(eng, n):
            if n in (W_CMP, W_CMP + 1):
                eng.wait_ge(aux_full, AUX["cmp_raw"] + 1)
            elif n < W_G01:
                eng.wait_ge(pmm_full, J_SMALL + 2 * (n - W_SMALL) + 2)
            elif n < W_BR:
                eng.wait_ge(pmm_full, J_GATE + 2 * (n - W_G01 - (2 if n > W_CMP else 0)) + 2)
            elif n < W_Q:
                last = BR_ORDER.index((1 if n == W_BR else 3, 1))
                eng.wait_ge(pmm_full, J_BR + 2 * last + 2)
            else:
                eng.wait_ge(pmm_full, J_Q + 2 * (n - W_Q) + 3)

        heads = ([(0, T_FQ + i // 2, i % 2, T_FK + i // 2, i % 2, C_FV + DH * i) for i in range(FOX_H)]
                 + [(1 + i // 2, T_DQ + i // 2, i % 2, T_DK + i // 2, i % 2, C_DV + DH * i) for i in range(DIL_H)]
                 + [(0, T_NQR + i // 2, i % 2, T_KS, i % 2, C_NVS) for i in range(NSA_H)]
                 + [(0, T_NQR + i // 2, i % 2, T_KW, i % 2, C_NVW) for i in range(NSA_H)])
        SLC0, WIN0 = FOX_H + DIL_H, FOX_H + DIL_H + NSA_H

        with nc.Fori(0, DEPTH) as l:
            with nc.Block() as block:

                @block.sync
                def _(sp):
                    def load(n, dst, src):
                        sp.dma_start(dst, src).then_inc(w_landed[n % WSLOTS], 16)

                    def room(n):
                        if n >= WSLOTS:
                            used_up(sp, n - WSLOTS)

                    def cols(n, w, c0, width):
                        room(n)
                        load(n, w_at(n)[:, 0:KC * width].rearrange("p (k c) -> p k c", k=KC),
                             w[l].rearrange("(k p) c -> p k c", p=P)[:, :, c0:c0 + width])

                    cols(0, w_in, 0, SCW)
                    sp.dma_start(rawp[0:4, 0, :], lru_conv_w[l]).then_inc(p_landed, 16)
                    for r, v in enumerate((lru_conv_b, lru_b_a, lru_b_x, lru_lambda)):
                        sp.dma_start(rawp[4 + r:5 + r, 0, :], v[l].partition_broadcast(1)).then_inc(p_landed, 16)
                    for t, v in enumerate((nsa_pe_k, nsa_pe_v)):
                        sp.dma_start(rawp[:, 1, t * P:(t + 1) * P],
                                     v[l].rearrange("(a b) d -> a (b d)", b=2)).then_inc(p_landed, 16)
                    sp.dma_start(rsub[:, :, :], peer_sub_keys[l].rearrange("a n d -> n a d")).then_inc(p_landed, 16)
                    cols(1, w_in, SCW, SCW)
                    for t, v in enumerate((lru_w_a, lru_w_x)):
                        for half in range(2):
                            sp.dma_start(wab[DH * half:DH * half + DH, t, :, DH * half:DH * half + DH],
                                         v[l].rearrange("(g a) c d -> a c g d", a=2)[half]).then_inc(p_landed, 16)
                    for c in range(2):
                        sp.dma_start(w2kd[:, :, c * DH:(c + 1) * DH],
                                     nsa_w2_k[l].rearrange("(a p) d -> p a d", p=P)).then_inc(p_landed, 16)
                    sp.dma_start(w2v[:, :, :], nsa_w2_v[l].rearrange("(a p) d -> p a d", p=P)).then_inc(p_landed, 16)
                    sp.dma_start(bfb[:, :], fox_b_f[l].partition_broadcast(P)).then_inc(p_landed, 16)
                    for c in range(2, SCH):
                        cols(c, w_in, c * SCW, SCW)
                    for c in range(2):
                        cols(gate_load(c), w_in, SMALL + c * GCW, GCW)
                    for t, v in enumerate((nsa_w1_k, nsa_w1_v)):
                        room(W_CMP + t)
                        load(W_CMP + t, w_at(W_CMP + t).rearrange("p (k c) -> p k c", k=16),
                             v[l].rearrange("(k p) c -> p k c", p=P))
                    for c in range(2, GCH):
                        cols(gate_load(c), w_in, SMALL + c * GCW, GCW)
                    for n, pair in ((W_BR, ((w_br_lru, 2), (w_br_fox, 2))), (W_BR + 1, ((w_br_dil, 1), (w_br_nsa, 2)))):
                        room(n)
                        at = 0
                        for v, k in pair:
                            load(n, w_at(n)[:, at:at + k * D].rearrange("p (k c) -> p k c", k=k),
                                 v[l].rearrange("(k p) c -> p k c", p=P))
                            at += k * D
                    cols(W_Q, peer_w_q, 0, 512)
                    sp.wait_ge(o_done, HEADS)
                    for c in range(2):
                        sp.dma_start(w_out_at[c], w_out[l].rearrange("(k p) c -> p k c", p=P)[
                            :, :, 512 * c:512 * c + 512]).then_inc(wo_landed[c], 16)
                    for c in range(1, 3):
                        cols(W_Q + c, peer_w_q, 512 * c, 512)
                        if c == 2:
                            sp.wait_ge(aux_full, AUX["mT3"] + 1)
                            sp.dma_start(gain, norm2_g[l].partition_broadcast(P)).then_inc(g_landed, 16)
                            for k in range(KC):
                                for e in range(2):
                                    sp.dma_start(w_q3_at[k][e], peer_w_q[l].rearrange("(k p) c -> k p c", p=P)[
                                        k, :, 1536 + 256 * e:1536 + 256 * e + 256]).then_inc(wq3_landed, 16)

                    sp.wait_ge(h_done, 2 * NB)
                    sp.dma_start(gain, gains[l + 1].partition_broadcast(P)).then_inc(g_landed, 16)
                    sp.wait_ge(g_landed, 32)

                N_PARAMS = 5 + 2 + 1 + 4 + 2 + 1 + 1

                @block.tensor
                def _(pe):
                    mmul, tp = nc.tensor.matmul, nc.tensor.transpose

                    def aux_bank(name):
                        n = AUX[name]
                        if n >= 2:
                            pe.wait_ge(aux_done, n - 1)
                        return paux[:, n % 2, :]

                    def turn_h(name, src, b, k0):
                        bank = aux_bank(name)
                        for k in range(4):
                            last = tp(bank[:, k * P:(k + 1) * P], src[:, b, (k0 + k) * P:(k0 + k + 1) * P], ident[:, :])
                        last.then_inc(aux_full, 1)

                    def turn_groups(name, parts):
                        bank = aux_bank(name)
                        for k, src in enumerate(parts):
                            last = tp(bank[:, k * P:(k + 1) * P], src, ident[:, :])
                        last.then_inc(aux_full, 1)

                    def project(j, n, b, width):
                        w_wait(pe, n)
                        multiply(j, w_at(n)[:, 0:KC * width].rearrange("p (k c) -> p k c", k=KC), b, width)

                    def project_out(b, half):
                        pe.wait_ge(wo_landed[half], 16)
                        multiply(J_OUTS[2 * b + half], w_out_at[half], b, 512)

                    def multiply(j, w, b, width):
                        pmm_free(pe, j)
                        for k in range(KC):
                            last = mmul(pmm[:, j % 2, 0:width], hT[:, k, b * P:(b + 1) * P], w[:, k, :],
                                        start=(k == 0), stop=(k == KC - 1))
                        last.then_inc(pmm_full, 1)

                    def turn_params():
                        pe.wait_ge(p_landed, 16 * N_PARAMS)
                        bank = aux_bank("params")
                        for g in range(2):
                            tp(bank[:, 8 * g:8 * g + 8], rawp[0:8, 0, g * P:(g + 1) * P], ident[0:8, 0:8])
                        for t in range(2):
                            last = tp(bank[:, 16 + 16 * t:32 + 16 * t], rawp[:, 1, t * P:(t + 1) * P], ident[0:16, 0:16])
                        last.then_inc(aux_full, 1)
                        turn_groups("subkeys", [rsub[:, a, :] for a in range(PK)])

                    def gate_job(m):
                        project(J_GATE + m, gate_load(m // 2), m % 2, GCW)

                    for b in range(NB):
                        pe.wait_ge(h_done, b + 1)
                        for q in range(2):
                            turn_h(f"hT{2 * b + q}", h, b, 4 * q)
                    pe.wait_ge(aux_done, AUX["hT3"] + 1)
                    for c in range(SCH):
                        for b in range(NB):
                            project(J_SMALL + 2 * c + b, W_SMALL + c, b, SCW)
                        if c == 2:
                            turn_params()

                    gate_job(0)
                    pe.wait_ge(pmm_dve, 2 * SCH)
                    for b in range(NB):
                        turn_groups(f"J0b{b}", [proj[:, b, c:c + P] for c in (C_FQ, C_FQ + P, C_NQ, C_NQ + P)])
                    for b in range(NB):
                        turn_groups(f"J1b{b}", [proj[:, b, c:c + P] for c in (C_FK, C_FK + P, C_LX, C_LX + P)])
                    pe.wait_ge(dup_done, 4)
                    for b in range(NB):
                        turn_groups(f"J2b{b}", [proj[:, b, C_LG:C_LG + P], proj[:, b, C_LG + P:C_LG + 2 * P],
                                                dup[:, b, 0:P], dup[:, b, P:2 * P]])
                    gate_job(1)
                    pe.wait_ge(fsp_done, 1)
                    bank = aux_bank("forget")
                    for b in range(NB):
                        last = tp(bank[0:4, b * P:(b + 1) * P], Y[:, 5, 4 * b:4 * b + 4], ident[:, :])
                    last.then_inc(aux_full, 1)
                    gate_job(2)
                    gate_job(3)
                    pe.wait_ge(xc_done, 1)
                    for t, name in enumerate(("ZA", "ZX")):
                        bank = aux_bank(name)
                        for g in range(2):
                            last = mmul(bank[:, g * SEQ:(g + 1) * SEQ], wab[:, t, g, :], xc[:, g, :], start=True, stop=True)
                        last.then_inc(aux_full, 1)
                    pe.wait_ge(rope_done, NB)
                    for b in range(NB):
                        turn_groups(f"J3b{b}", [rope_o[:, b, c:c + P] for c in (0, P, 2 * P, 768)])
                    for b in range(NB):
                        turn_groups(f"J4b{b}", [rope_o[:, b, 768 + P:768 + 2 * P]])
                    for b in range(NB):
                        turn_groups(f"J5b{b}", [rope_o[:, b, c:c + P] for c in (384, 384 + P, 384 + 2 * P, 1024)])
                    for b in range(NB):
                        turn_groups(f"J6b{b}", [rope_o[:, b, 1152:1280]])
                    pe.wait_ge(cin_done, 1)
                    bank = aux_bank("cmp_raw")
                    for t in range(2):
                        w_wait(pe, W_CMP + t)
                        w = w_at(W_CMP + t).rearrange("p (k c) -> p k c", k=16)
                        for k in range(16):
                            last = mmul(bank[0:N_CMP, t * CMP_HID:(t + 1) * CMP_HID], cin[:, t, k, :], w[:, k, :],
                                        start=(k == 0), stop=(k == 15))
                    last.then_inc(aux_full, 1)

                    def scores(i):
                        m, gq, hq, gk, hk, _ = heads[i]
                        if i >= 2:
                            pe.wait_ge(exp_done, 2 * (i - 1))
                        bank = psc[:, i % 2, 0:384]
                        fox = i < FOX_H
                        mmul(bank, ident_b[:, :], masks[:, m, :], start=True, stop=False, skip_group_check=True)
                        for b in range(NB):
                            o = bank[:, 0:P] if b == 0 else bank[:, P:384]
                            nk = (b + 1) * P
                            last = mmul(o, T[DH * hq:DH * hq + DH, gq, b * P:(b + 1) * P],
                                        T[DH * hk:DH * hk + DH, gk, 0:nk], start=False, stop=not fox,
                                        skip_group_check=True)
                            if fox:
                                mmul(o, cumf[0:4, b * P:(b + 1) * P], E4(1, i, nk), start=False, stop=False,
                                     skip_group_check=True)
                                last = mmul(o, pick[0:4, 0, i, :], cumf[0:4, 0:nk], start=False, stop=True,
                                            skip_group_check=True)
                        last.then_inc(sc_full, 1)

                    def E4(s, i, nk):
                        return pick[0:4, s, i, :] if nk == P else pick[0:4, s, i, :].unsqueeze(1).to_broadcast([4, 2, P])

                    def turn_probs(i):
                        pe.wait_ge(exp_done, 2 * (i + 1))
                        if i >= 1:
                            pe.wait_ge(pt_done, i)
                        for c in range(3):
                            last = tp(ppo[:, 0, c * P:(c + 1) * P], prob[:, i % 2, c * P:(c + 1) * P], ident[:, :])
                        last.then_inc(pt_full, 1)

                    def weighted(i):
                        pe.wait_ge(pt_done, i + 1)
                        if i >= 2:
                            pe.wait_ge(o_done, i - 1)
                        vc = heads[i][5]
                        o = ppo[:, 1, (i % 2) * P:(i % 2) * P + P]
                        mmul(o[:, 0:DH], probT[:, i % 2, 0:P], proj[:, 0, vc:vc + DH], start=True, stop=True)
                        mmul(o[:, DH:P], probT[:, i % 2, P:2 * P], proj[:, 0, vc:vc + DH], start=True, stop=False)
                        mmul(o[:, DH:P], probT[:, i % 2, 2 * P:384], proj[:, 1, vc:vc + DH],
                             start=False, stop=True).then_inc(o_full, 1)

                    branch_at = ((W_BR, 0, 2, 0), (W_BR, 2 * D, 2, 2), (W_BR + 1, 0, 1, 4), (W_BR + 1, D, 2, 5))

                    def branch(idx, b, halves=(0, 1)):
                        n, off, ks, t0 = branch_at[idx]
                        for half in halves:
                            j = J_BR + 2 * BR_ORDER.index((idx, b)) + half
                            pmm_free(pe, j)
                            w = w_at(n)[:, off:off + ks * D].rearrange("p (k c) -> p k c", k=ks)
                            for k in range(ks):
                                last = mmul(pmm[:, j % 2, :], oT[:, t0 + k, b * P:(b + 1) * P],
                                            w[:, k, 512 * half:512 * half + 512], start=(k == 0), stop=(k == ks - 1))
                            last.then_inc(pmm_full, 1)

                    pe.wait_ge(cum_done, 1)
                    pe.wait_ge(aux_done, AUX["J6b1"] + 1)
                    scores(0)
                    pe.wait_ge(aux_done, AUX["cmp_raw"] + 1)
                    bank = aux_bank("cmp_hidden")
                    for g in range(4):
                        last = tp(bank[:, 16 * g:16 * g + N_CMP], hid_raw[:, g * P:(g + 1) * P],
                                  ident[0:N_CMP, 0:N_CMP])
                    last.then_inc(aux_full, 1)
                    for i in range(HEADS + 1):
                        if i < HEADS:
                            if i + 1 < HEADS:
                                scores(i + 1)
                            for m in gate_jobs_at(i):
                                gate_job(m)
                        if i >= HEADS - 1:
                            if i == HEADS - 1:
                                pe.wait_ge(lru_done, 1)
                                w_wait(pe, W_BR)
                            branch(0, 0, (i - HEADS + 1,))
                        if i >= 1:
                            weighted(i - 1)
                        if i < HEADS:
                            turn_probs(i)
                        if i == 2:
                            pe.wait_ge(hrep_done, 1)
                            bank = aux_bank("cmp_kv")
                            for hh in range(2):
                                mmul(bank[:, 0:N_CMP], w2kd[:, hh, :], hg[:, 2, hh, 0:N_CMP], start=(hh == 0), stop=(hh == 1))
                            for hh in range(2):
                                last = mmul(bank[:, DH:2 * DH], hrep[:, hh, :, :].rearrange("p a b -> p (a b)"), w2v[:, hh, :],
                                            start=(hh == 0), stop=(hh == 1))
                            last.then_inc(aux_full, 1)
                        if i == 3:
                            pe.wait_ge(aux_done, AUX["cmp_kv"] + 1)
                            bank = aux_bank("cmp_scores")
                            for r in (0, DH):
                                for b in range(NB):
                                    for q in range(r // DH, NSA_H, 2):
                                        o = 16 * (NSA_H * b + q)
                                        last = mmul(bank[:, o:o + N_CMP], T[r:r + DH, T_NQ + q // 2, b * P:(b + 1) * P],
                                                    kcT[r:r + DH, 0:N_CMP], start=True, stop=True)
                                if r == 0:
                                    last.then_inc(pe_half, 1)
                                    pe.wait_ge(pe_half, 1)
                            last.then_inc(aux_full, 1)
                        if i == 6:
                            pe.wait_ge(pc_done, 1)
                            turn_groups("cmp_pT", [pc[:, b, :, :].rearrange("p a c -> p (a c)") for b in range(NB)])
                        if i == 7:
                            pe.wait_ge(aux_done, AUX["cmp_pT"] + 1)
                            bank = aux_bank("cmp_out")
                            for b in range(NB):
                                last = mmul(bank[:, b * SEQ:(b + 1) * SEQ], pcT[:, b * P:(b + 1) * P],
                                            vbd[:, :, :].rearrange("p h d -> p (h d)"), start=True, stop=True)
                            last.then_inc(aux_full, 1)
                        if i == 9:
                            pe.wait_ge(o_done, FOX_H)
                            turn_groups("foxT", [o_fox[:, b, g * P:(g + 1) * P] for g in range(2) for b in range(NB)])
                        if i == 15:
                            pe.wait_ge(od_done, 1)
                            turn_groups("dilT", [o_dilm[:, b, :, :].rearrange("p h d -> p (h d)") for b in range(NB)])

                    pe.wait_ge(aux_done, AUX["foxT"] + 1)
                    branch(1, 0)
                    w_wait(pe, W_BR + 1)
                    pe.wait_ge(aux_done, AUX["dilT"] + 1)
                    branch(2, 0)
                    pe.wait_ge(o_done, HEADS)
                    turn_groups("nsaT", [o_nsa[:, b, 2 * g:2 * g + 2, :].rearrange("p h d -> p (h d)")
                                         for g in range(2) for b in range(NB)])
                    branch(0, 1)
                    pe.wait_ge(aux_done, AUX["nsaT"] + 1)
                    branch(3, 0)
                    branch(1, 1)
                    branch(2, 1)
                    def turn_merged(b):
                        pe.wait_ge(m_done, b + 1)
                        for q in range(2):
                            turn_h(f"mT{2 * b + q}", merged, b, 4 * q)

                    turn_merged(0)
                    branch(3, 1)
                    pe.wait_ge(aux_done, AUX["mT1"] + 1)
                    project_out(0, 0)
                    turn_merged(1)
                    project_out(0, 1)

                    def turn_normed(b):
                        pe.wait_ge(h_done, NB + b + 1)
                        for q in range(2):
                            turn_h(f"h2T{2 * b + q}", h, b, 4 * q)

                    def queries(hd, blocks=(0, 1)):
                        j, n = J_Q00 if blocks == (0,) else J_Q + hd + 1, W_Q + hd // 2
                        pmm_free(pe, j)
                        if hd < 6:
                            w_wait(pe, n)
                            ring = w_at(n).rearrange("p (k c) -> p k c", k=KC)
                            w = [ring[:, k, (hd % 2) * 256:(hd % 2) * 256 + 256] for k in range(KC)]
                        else:
                            pe.wait_ge(wq3_landed, 2 * KC * 16)
                            w = [w_q3_at[k][hd % 2] for k in range(KC)]
                        t0, t1 = blocks[0] * P, (blocks[-1] + 1) * P
                        for a in range(PK):
                            for k in range(KC):
                                last = mmul(pmm[:, j % 2, a * SEQ + t0:a * SEQ + t1], w[k][:, a * P:a * P + P], hT[:, k, t0:t1],
                                            start=(k == 0), stop=(k == KC - 1))
                        last.then_inc(pmm_full, 1)

                    def key_scores(u, r):
                        pe.wait_ge(qst_done, u + 1)
                        pe.wait_ge(es_used, u + 1)
                        for a in range(PK):
                            last = mmul(psc[:, r, a * P:(a + 1) * P], qst[:, r, a, :], subT[:, a, :],
                                        start=True, stop=True)
                        last.then_inc(es_full, 1)

                    def seed(b):
                        for half in range(2):
                            mmul(paux[:, half, :], ident[:, :], x[:, b, 512 * half:512 * half + 512],
                                 start=True, stop=True)

                    def sums(u, count=TOPK):
                        for k in range(count):
                            pe.wait_ge(row_landed[k], (l * UNITS + u) * 32 + 32)
                            pe.wait_ge(diag_done, u * TOPK + k + 1)
                            for half in range(2):
                                last = mmul(paux[:, half, :], diag[:, k % NDIAG, :], rows[:, k, 512 * half:512 * half + 512],
                                            start=False, stop=True, skip_group_check=True)
                            last.then_inc(sums_done, 1)

                    turn_normed(0)
                    pe.wait_ge(aux_done, AUX["h2T1"] + 1)
                    queries(0, (0,))
                    key_scores(0, 0)
                    for half in range(2):
                        project_out(1, half)
                    turn_normed(1)
                    pe.wait_ge(aux_done, AUX["h2T3"] + 1)
                    queries(0, (1,))
                    queries(1)
                    key_scores(1, 1)
                    seed(0)
                    queries(2)
                    queries(3)
                    key_scores(2, 0)
                    sums(0)
                    key_scores(3, 1)
                    queries(4)
                    queries(5)
                    key_scores(4, 0)
                    sums(1)
                    queries(6)
                    queries(7)
                    key_scores(5, 1)
                    with pe.Fori(1, UNITS // 4) as p:
                        for r in range(2):
                            sums(2 * p + r)
                            key_scores(2 * p + r + 4, r)
                    pe.wait_ge(pe_back, 1)
                    seed(1)
                    with pe.Fori(UNITS // 4, UNITS // 2 - 2) as p:
                        for r in range(2):
                            sums(2 * p + r)
                            key_scores(2 * p + r + 4, r)
                    for u in range(UNITS - 4, UNITS - 1):
                        sums(u)
                    sums(UNITS - 1, PE_SHARE)

                @block.scalar
                def _(act):
                    A = nc.scalar.activation
                    steps = [0]

                    def chain(ins):
                        steps[0] += 1
                        ins.then_inc(act_step, 1)
                        act.wait_ge(act_step, steps[0])

                    def bank_of(name):
                        act.wait_ge(aux_full, AUX[name] + 1)
                        return paux[:, AUX[name] % 2, :]

                    def std(first, blocks=(0, 1)):
                        for b in blocks:
                            if not first:
                                act.wait_ge(pmm_dve, J_GATE + 16 + 2 * b + 2)
                            chain(A(h[:, b, :], x[:, b, :], ACT.Square, accum_out=stat[:, b:b + 1]))
                            A(stat[:, 2 + b:3 + b], stat[:, b:b + 1], ACT.Sqrt, bias=eps[:, :], scale=1.0 / D).then_inc(std_done, 1)

                    def take_hT(prefix, scale, jobs=(0, 1, 2, 3)):
                        for n in jobs:
                            b, q = n // 2, n % 2
                            bank = bank_of(f"{prefix}{n}")
                            A(hT[:, 4 * q:4 * q + 4, b * P:(b + 1) * P], bank.rearrange("p (k t) -> p k t", k=4),
                              ACT.Copy, scale=scale).then_inc(aux_done, 1)

                    def take(name, g0, n, b, scale=1.0):
                        bank = bank_of(name)
                        A(T[:, g0:g0 + n, b * P:(b + 1) * P], bank[:, 0:n * P].rearrange("p (k t) -> p k t", k=n),
                          ACT.Copy, scale=scale).then_inc(aux_done, 1)

                    def gate_tanh(m):
                        c, b = m // 2, m % 2
                        act.wait_ge(pmm_full, J_GATE + m + 1)
                        A(gate[:, b, c * GCW:(c + 1) * GCW], pmm[:, (J_GATE + m) % 2, :], ACT.Tanh,
                          scale=0.5).then_inc(pmm_act, 1)

                    def load_sqrt():
                        A(stat[:, 7:8], eps[:, :], ACT.Sqrt)

                    load_sqrt()
                    act.wait_ge(s_const, 5 * 16)
                    std(True)
                    take_hT("hT", 1.0)
                    bank = bank_of("params")
                    A(lp[:, :, :].rearrange("p g c -> p (g c)"), bank[:, 0:16], ACT.Copy)
                    A(peT[:, :, :].rearrange("p t c -> p (t c)"), bank[:, 16:48], ACT.Copy).then_inc(aux_done, 1)
                    bank = bank_of("subkeys")
                    A(subT[:, :, :].rearrange("p a n -> p (a n)"), bank[:, 0:PK * P], ACT.Copy).then_inc(aux_done, 1)
                    act.wait_ge(pmm_dve, 2 * SCH)
                    for b in range(NB):
                        for t, c in enumerate((C_NKC, C_NVC)):
                            A(dup[:, b, t * P:(t + 1) * P].rearrange("p (a d) -> p a d", a=2),
                              proj[:, b, c:c + DH].unsqueeze(1).to_broadcast([P, 2, DH]), ACT.Copy).then_inc(dup_done, 1)
                    A(ng[:, :, :, :].rearrange("p b h c -> p b (h c)"), proj[:, :, C_NG:C_NG + 12], ACT.Tanh,
                      scale=0.5).then_inc(ng_done, 1)
                    for b in range(NB):
                        take(f"J0b{b}", T_FQ, 4, b, 0.125)
                    for b in range(NB):
                        take(f"J1b{b}", T_FK, 4, b)
                    for b in range(NB):
                        take(f"J2b{b}", T_LG, 4, b)
                    act.wait_ge(sp_abs, 1)
                    A(Y[:, 2, :], Y[:, 1, :], ACT.Exp, scale=-1.0).then_inc(sp_exp, 1)
                    gate_tanh(0)
                    gate_tanh(1)
                    bank = bank_of("forget")
                    A(fl[0:4, :], bank[0:4, 0:SEQ], ACT.Copy).then_inc(aux_done, 1)
                    gate_tanh(2)
                    gate_tanh(3)
                    act.wait_ge(hb_done, 1)
                    for t, (name, dst_) in enumerate((("ZA", lb), ("ZX", ld))):
                        bank = bank_of(name)
                        for g in range(2):
                            last = A(dst_[:, g, :], bank[:, g * SEQ:(g + 1) * SEQ], ACT.Tanh,
                                     bias=lph[:, g, t:t + 1], scale=0.5)
                        last.then_inc(aux_done, 1)
                    for b in range(NB):
                        take(f"J3b{b}", T_DQ, 4, b, 0.125)
                    for b in range(NB):
                        take(f"J4b{b}", T_NQR + 1, 1, b, 0.125)
                    for b in range(NB):
                        take(f"J5b{b}", T_DK, 4, b)
                    for b in range(NB):
                        take(f"J6b{b}", T_KW, 1, b)
                    bank = bank_of("cmp_raw")
                    A(hid_raw, bank[0:N_CMP, 0:2 * CMP_HID], ACT.Copy).then_inc(aux_done, 1)
                    bank = bank_of("cmp_hidden")
                    A(hid[:, :, 0:N_CMP], bank[:, 0:64].rearrange("p (k c) -> p k c", k=4)[:, :, 0:N_CMP],
                      ACT.Copy).then_inc(aux_done, 1)

                    for i in range(HEADS):
                        act.wait_ge(mx_done, i + 1)
                        if i >= 2:
                            act.wait_ge(pt_full, i - 1)
                        A(prob[:, i % 2, 0:P], psc[:, i % 2, 0:P], ACT.Exp, bias=nmax[:, i, 0:1],
                          accum_out=lsum[:, i, 0:1]).then_inc(exp_done, 1)
                        A(prob[:, i % 2, P:384], psc[:, i % 2, P:384], ACT.Exp, bias=nmax[:, i, 1:2],
                          accum_out=lsum[:, i, 1:2]).then_inc(exp_done, 1)
                        for m in gate_jobs_at(i):
                            gate_tanh(m)
                        if i == 0:
                            act.wait_ge(la_done, 1)
                            A(le[:, :, :], la[:, :, :], ACT.Tanh).then_inc(dec_done, 1)
                            act.wait_ge(dec_done, 1)
                            A(la[:, :, :], la[:, :, :], ACT.Exp).then_inc(dec_done, 1)
                            act.wait_ge(hgin_done, 1)
                            A(hg[:, 1, :, 0:N_CMP], hg[:, 0, :, 0:N_CMP], ACT.Tanh, scale=GELU_S).then_inc(hgt_done, 1)
                        if i == 2:
                            act.wait_ge(ysq_done, 1)
                            A(lb[:, :, :], lb[:, :, :], ACT.Sqrt, scale=0.5).then_inc(root_done, 1)
                            bank = bank_of("cmp_kv")
                            A(kcT[:, 0:N_CMP], bank[:, 0:N_CMP], ACT.Copy, scale=0.5)
                            for q in range(NSA_H):
                                last = A(vbd[32 * q:32 * q + 32, q, :], bank[32 * q:32 * q + 32, DH:2 * DH],
                                         ACT.Copy, scale=0.5)
                            last.then_inc(aux_done, 1)
                        if i == 3:
                            bank = bank_of("cmp_scores")
                            A(lc[:, :, :, 0:N_CMP], bank[:, 0:P].rearrange("p (b h c) -> p b h c", b=NB, h=NSA_H)[:, :, :, 0:N_CMP],
                              ACT.Copy).then_inc(aux_done, 1)
                            act.wait_ge(gin_done, 1)
                            A(ld[:, :, :], le[:, :, :], ACT.Tanh, scale=GELU_S).then_inc(gth_done, 1)
                        if i == 5:
                            act.wait_ge(lcd_done, 1)
                            A(lc[:, :, :, 0:N_CMP], lc[:, :, :, 0:N_CMP], ACT.Exp).then_inc(lce_done, 1)
                        if i == 6:
                            bank = bank_of("cmp_pT")
                            A(pcT[:, :], bank[:, 0:SEQ], ACT.Copy).then_inc(aux_done, 1)
                        if i == 7:
                            bank = bank_of("cmp_out")
                            A(oc[:, :, :, :].rearrange("p b h d -> p (b h d)"), bank, ACT.Copy).then_inc(aux_done, 1)
                        if i == 9:
                            bank = bank_of("foxT")
                            A(oT[:, 2:4, :].rearrange("p g t -> p (g t)"), bank, ACT.Copy).then_inc(aux_done, 1)
                        if i == 15:
                            bank = bank_of("dilT")
                            A(oT[:, 4, :], bank[:, 0:SEQ], ACT.Copy).then_inc(aux_done, 1)
                        if i == 12:
                            act.wait_ge(dw_in, 1)
                            A(dst[:, 1, :, :], dst[:, 0, :, :], ACT.Exp).then_inc(dw_exp, 1)

                    bank = bank_of("nsaT")
                    A(oT[:, 5:7, :].rearrange("p g t -> p (g t)"), bank, ACT.Copy).then_inc(aux_done, 1)
                    take_hT("mT", 0.5)
                    load_sqrt()
                    std(False, (0,))
                    take_hT("h2T", 1.0, (0, 1))

                    def take_q(hd, blocks=(0, 1)):
                        j = J_Q00 if blocks == (0,) else J_Q + hd + 1
                        act.wait_ge(pmm_full, j + 1)
                        for a in range(PK):
                            for b in blocks:
                                last = A(qT[:, b * PH + hd, a, :], pmm[:, j % 2, a * SEQ + b * P:a * SEQ + b * P + P], ACT.Copy)
                        last.then_inc(pmm_act, 1)
                        act.wait_ge(pmm_act, 2 * GCH + (1 if blocks == (0,) else hd + 2))

                    def stage(u, r, first=False):
                        if not first:
                            act.wait_ge(es_full, u - 1)
                        A(qst[:, r, :, :], qT[:, u, :, :], ACT.Copy).then_inc(qst_done, 1)

                    def softmax_exp(u, r):
                        act.wait_ge(top_done, u + 1)
                        A(sexp[:, r, :], sdiff[:, r, :], ACT.Exp, accum_out=sl[:, r, :]).then_inc(sexp_done, 1)

                    def gelu_tanh(u, r):
                        act.wait_ge(gin2_done, u + 1)
                        A(gt[:, r, :], gin[:, r, :], ACT.Tanh, scale=GELU_S).then_inc(gt2_done, 1)

                    def diagonals(u, r, count=TOPK):
                        act.wait_ge(w_ready, u + 1)
                        for k in range(count):
                            act.wait_ge(sums_done, u * TOPK + k + 1 + RING - NDIAG)
                            A(diag[:, k % NDIAG, :], ident[:, :], ACT.Copy, scale=wv[:, r, k:k + 1]).then_inc(diag_done, 1)

                    def into_psum(b):
                        A(ppo[:, :, :].rearrange("p a c -> p (a c)"), h[:, b, :], ACT.Copy).then_inc(pe_in, 1)
                        act.wait_ge(pe_in, b + 1)

                    def back():
                        act.wait_ge(sums_done, PH * TOPK + RING)
                        A(x[:, 0, :], paux[:, :, :].rearrange("p a c -> p (a c)"), ACT.Copy).then_inc(pe_back, 1)

                    act.wait_ge(h_done, NB + 1)
                    into_psum(0)
                    take_q(0, (0,))
                    stage(0, 0, True)
                    softmax_exp(0, 0)
                    std(False, (1,))
                    take_hT("h2T", 1.0, (2, 3))
                    take_q(0, (1,))
                    take_q(1)
                    stage(1, 1, True)
                    take_q(2)
                    stage(2, 0)
                    gelu_tanh(0, 0)
                    take_q(3)
                    diagonals(0, 0)
                    stage(3, 1)
                    softmax_exp(1, 1)
                    take_q(4)
                    take_q(5)
                    stage(4, 0)
                    softmax_exp(2, 0)
                    gelu_tanh(1, 1)
                    diagonals(1, 1)
                    take_q(6)
                    take_q(7)
                    stage(5, 1)
                    softmax_exp(3, 1)

                    def unit(u, r):
                        gelu_tanh(u, r)
                        diagonals(u, r)
                        stage(u + 4, r)
                        softmax_exp(u + 2, r)

                    with act.Fori(1, UNITS // 4 - 1) as p:
                        unit(2 * p, 0)
                        unit(2 * p + 1, 1)
                    unit(PH - 2, 0)
                    gelu_tanh(PH - 1, 1)
                    act.wait_ge(dots_done, PH * TOPK)
                    into_psum(1)
                    diagonals(PH - 1, 1)
                    stage(PH + 3, 1)
                    softmax_exp(PH + 1, 1)
                    back()
                    with act.Fori(UNITS // 4, UNITS // 2 - 2) as p:
                        unit(2 * p, 0)
                        unit(2 * p + 1, 1)
                    for u in range(UNITS - 4, UNITS):
                        gelu_tanh(u, u % 2)
                        diagonals(u, u % 2, TOPK if u < UNITS - 1 else PE_SHARE)
                        if u + 2 < UNITS:
                            softmax_exp(u + 2, u % 2)

                @block.gpsimd
                def _(pool):
                    pool.wait_ge(pmm_dve, J_GATE + 16)
                    pool.wait_ge(pmm_full, J_OUTS[2] + 1)

                    def gather(p, r):
                        pool.wait_ge(top_done, 2 * p + r + 1)
                        pool.sem_inc(pool_held, 1)
                        nc.gpsimd.tensor_copy(gidx[:, r, :], eidx[:, r, :]).then_inc(idx_taken, 1)
                        pool.wait_ge(idx_taken, 2 * p + r + 1)
                        for t, table in enumerate((peer_u, peer_v)):
                            for k in range(TOPK):
                                pool.wait_ge((sums_done, dots_done)[t], (2 * p + r) * TOPK + k + 1)
                                pool.sem_inc(pool_held, 1)
                                nc.gpsimd.indirect_dma_start(
                                    out=rows[:, k, :], out_offset=None,
                                    in_=table.rearrange("l e d -> (l e) d"),
                                    in_offset=bass.IndirectOffsetOnAxis(ap=gidx[:, r, k:k + 1], axis=0),
                                ).then_inc(row_landed[k], 16)

                    with pool.Fori(0, UNITS // 2) as p:
                        gather(p, 0)
                        gather(p, 1)

                @block.vector
                def _(dve):
                    V = nc.vector
                    steps = [0]
                    TT, TS, STT = V.tensor_tensor, V.tensor_scalar, V.scalar_tensor_tensor

                    def chain(ins):
                        steps[0] += 1
                        ins.then_inc(dve_step, 1)
                        dve.wait_ge(dve_step, steps[0])

                    def norm(n0, g_count, blocks=(0, 1)):
                        if g_count:
                            dve.wait_ge(g_landed, 16 * g_count)
                        for b in blocks:
                            dve.wait_ge(std_done, n0 + b + 1)
                            chain(V.reciprocal(stat[:, 4 + b:5 + b], stat[:, 2 + b:3 + b]))
                            STT(h[:, b, :], x[:, b, :], stat[:, 4 + b:5 + b], gain, ALU.mult,
                                ALU.mult).then_inc(h_done, 1)

                    dve.wait_ge(s_const, 5 * 16)
                    norm(0, 0)

                    def rope_part(b, src, n, dst):
                        s = proj[:, b, src:src + n * DH].rearrange("p (n t d) -> p n t d", n=n, t=2)
                        t = rope_t[:, 0:n * DH].rearrange("p (n t d) -> p n t d", n=n, t=2)
                        o = dst.rearrange("p (n t d) -> p n t d", n=n, t=2)
                        sn = rope_c[:, b, 1, :].rearrange("p (t d) -> p t d", t=2)
                        TT(t[:, :, 0, :], s[:, :, 1, :], sn[:, 0, :].unsqueeze(1).to_broadcast([P, n, 32]), ALU.mult)
                        TT(t[:, :, 1, :], s[:, :, 0, :], sn[:, 1, :].unsqueeze(1).to_broadcast([P, n, 32]), ALU.mult)
                        chain(TT(o.rearrange("p n t d -> p n (t d)"), s.rearrange("p n t d -> p n (t d)"),
                                 rope_c[:, b, 0, :].unsqueeze(1).to_broadcast([P, n, DH]), ALU.mult))
                        of, tf = o.rearrange("p n t d -> p (n t d)"), t.rearrange("p n t d -> p (n t d)")
                        chain(TT(of, of, tf, ALU.add))

                    for c in range(SCH):
                        for b in range(NB):
                            j = 2 * c + b
                            dve.wait_ge(pmm_full, j + 1)
                            V.tensor_copy(proj[:, b, c * SCW:(c + 1) * SCW], pmm[:, j % 2, 0:SCW]).then_inc(pmm_dve, 1)
                        if c == 5:
                            dve.wait_ge(pmm_dve, 12)
                            for b in range(NB):
                                rope_part(b, C_DQ, DIL_H, rope_o[:, b, 0:384])
                                rope_part(b, C_DK, DIL_H, rope_o[:, b, 384:768])
                        if c == 4:
                            dve.wait_ge(p_landed, 16 * N_PARAMS)
                            dve.wait_ge(pmm_dve, 10)
                            dve.wait_ge(aux_done, AUX["params"] + 1)
                            y = Y[:, 0, :]
                            TT(y[:, 0:8].rearrange("p (b h) -> p b h", b=NB), proj[:, :, C_FF:C_FF + 4],
                               bfb[:, :].unsqueeze(1).to_broadcast([P, NB, 4]), ALU.add)
                            chain(V.tensor_copy(y[:, 8:10], lp[:, :, 7]))
                            chain(TS(Y[:, 3, :], y, -1.0, None, ALU.mult))
                            TT(Y[:, 1, :], y, Y[:, 3, :], ALU.max).then_inc(sp_abs, 1)
                            TS(Y[:, 5, :], Y[:, 3, :], 0.0, None, ALU.max)
                            TS(lph[:, :, :], lp[:, :, 5:7], 0.5, None, ALU.mult).then_inc(hb_done, 1)
                    dve.wait_ge(pmm_dve, 2 * SCH)
                    dve.wait_ge(sp_exp, 1)
                    e, z, z2, acc = Y[:, 2, :], Y[:, 3, :], Y[:, 4, :], Y[:, 1, :]
                    chain(TS(z, e, 2.0, None, ALU.add))
                    chain(V.reciprocal(z, z))
                    chain(TT(z, z, e, ALU.mult))
                    chain(TT(z2, z, z, ALU.mult))
                    chain(TS(acc, z2, 1.0 / 17, None, ALU.mult))
                    for n in (15, 13, 11, 9, 7, 5, 3):
                        chain(STT(acc, acc, 1.0 / n, z2, ALU.add, ALU.mult))
                    chain(STT(acc, acc, 1.0, z, ALU.add, ALU.mult))
                    STT(Y[:, 5, :], acc, 2.0, Y[:, 5, :], ALU.mult, ALU.add).then_inc(fsp_done, 1)
                    dve.wait_ge(fsp_done, 1)
                    chain(TS(csp[:, :], Y[:, 5, 8:10], -4.0, None, ALU.mult))
                    dve.wait_ge(aux_done, AUX["J1b1"] + 1)
                    for g in range(2):
                        chain(TS(xc[:, g, :], T[:, T_LX + g, :], lp[:, g, 3:4], lp[:, g, 4:5], ALU.mult, ALU.add))
                        for s in range(1, 4):
                            last = STT(xc[:, g, s:SEQ], T[:, T_LX + g, 0:SEQ - s], lp[:, g, 3 - s:4 - s], xc[:, g, s:SEQ],
                                       ALU.mult, ALU.add)
                            if (g, s) != (1, 3):
                                chain(last)
                    last.then_inc(xc_done, 1)
                    dve.wait_ge(xc_done, 1)
                    dve.wait_ge(aux_done, AUX["J2b1"] + 1)
                    for t in range(2):
                        for half in range(2):
                            r = slice(DH * half, DH * half + DH)
                            src = T[r, T_KC + t, :].rearrange("p (c s u) -> p s u c", s=8, u=2)
                            for q in range(2):
                                last = TT(cin[r, t, 8 * q:8 * q + 8, :], src[:, :, half, q:q + N_CMP],
                                          peT[r, t, 8 * q:8 * q + 8].unsqueeze(2).to_broadcast([DH, 8, N_CMP]), ALU.add)
                    last.then_inc(cin_done, 1)
                    for b in range(NB):
                        rope_part(b, C_NQ, NSA_H, rope_o[:, b, 768:1024])
                        for t, c in enumerate((C_NKS, C_NKW)):
                            o = rope_o[:, b, 1024 + t * P:1024 + (t + 1) * P]
                            rope_part(b, c, 1, o[:, 0:DH])
                            last = V.tensor_copy(o[:, DH:P], o[:, 0:DH])
                            if t == 0:
                                chain(last)
                        last.then_inc(rope_done, 1)
                    dve.wait_ge(rope_done, 2)
                    ones4 = oT[0:4, 6, :]
                    chain(V.memset(ones4, 1.0))
                    dve.wait_ge(aux_done, AUX["forget"] + 1)
                    V.tensor_tensor_scan(cumf[0:4, :], ones4, fl[0:4, :], 0.0, ALU.mult, ALU.add).then_inc(cum_done, 1)
                    dve.wait_ge(cum_done, 1)
                    dve.wait_ge(aux_done, AUX["ZX"] + 1)
                    for g in range(2):
                        last = TS(la[:, g, :], lb[:, g, :], 1.0, csp[:, g:g + 1], ALU.add, ALU.mult)
                    last.then_inc(la_done, 1)
                    dve.wait_ge(aux_done, AUX["cmp_hidden"] + 1)
                    hv = hid[:, :, 0:N_CMP]
                    chain(TT(hg[:, 1, :, 0:N_CMP], hv, hv, ALU.mult))
                    chain(TS(hg[:, 1, :, 0:N_CMP], hg[:, 1, :, 0:N_CMP], GELU_C, 1.0, ALU.mult, ALU.add))
                    TT(hg[:, 0, :, 0:N_CMP], hg[:, 1, :, 0:N_CMP], hv, ALU.mult).then_inc(hgin_done, 1)

                    def head_max(i):
                        dve.wait_ge(sc_full, i + 1)
                        V.tensor_reduce(nmax[:, i, 0:1], psc[:, i % 2, 0:P], AX.X, ALU.max, negate=True)
                        V.tensor_reduce(nmax[:, i, 1:2], psc[:, i % 2, P:384], AX.X, ALU.max, negate=True).then_inc(mx_done, 1)

                    def take_probsT(i):
                        dve.wait_ge(pt_full, i + 1)
                        if i >= 2:
                            dve.wait_ge(o_full, i - 1)
                        V.tensor_copy(probT[:, i % 2, :], ppo[:, 0, 0:384]).then_inc(pt_done, 1)

                    def take_out(i):
                        dve.wait_ge(o_full, i + 1)
                        o = ppo[:, 1, (i % 2) * P:(i % 2) * P + P].rearrange("p (b d) -> p b d", b=NB)
                        if FOX_H <= i < SLC0:
                            V.tensor_copy(o_dil[:, :, i - FOX_H, :], o).then_inc(o_done, 1)
                            return
                        dve.wait_ge(exp_done, 2 * (i + 1))
                        chain(V.reciprocal(rl[:, i, :], lsum[:, i, :]))
                        if i < FOX_H:
                            for b in range(NB):
                                last = TS(o_fox[:, b, i * DH:(i + 1) * DH], o[:, b, :], rl[:, i, b:b + 1], None, ALU.mult)
                        else:
                            q = (i - SLC0) % NSA_H
                            chain(TT(rl[:, i, :], rl[:, i, :], ng[:, :, q, 1 if i < WIN0 else 2], ALU.mult))
                            for b in range(NB):
                                last = STT(o_nsa[:, b, q, :], o[:, b, :], rl[:, i, b:b + 1], o_nsa[:, b, q, :],
                                           ALU.mult, ALU.add)
                        last.then_inc(o_done, 1)
                        dve.wait_ge(o_done, i + 1)

                    def lru_root():
                        dve.wait_ge(dec_done, 1)
                        chain(TS(lb[:, :, :], le[:, :, :], -1.0, None, ALU.add))
                        chain(V.reciprocal(lb[:, :, :], lb[:, :, :]))
                        TT(lb[:, :, :], lb[:, :, :], le[:, :, :], ALU.mult).then_inc(ysq_done, 1)
                        dve.wait_ge(ysq_done, 1)
                        chain(STT(xc[:, :, :], ld[:, :, :], 1.0, xc[:, :, :], ALU.add, ALU.mult))
                        lg = T[:, T_LG:T_LG + 2, :]
                        chain(TT(le[:, :, :], lg, lg, ALU.mult))
                        chain(TS(le[:, :, :], le[:, :, :], GELU_C, 1.0, ALU.mult, ALU.add))
                        TT(le[:, :, :], le[:, :, :], lg, ALU.mult).then_inc(gin_done, 1)

                    def lru_scan():
                        dve.wait_ge(root_done, 1)
                        chain(TT(xc[:, :, :], xc[:, :, :], lb[:, :, :], ALU.mult))
                        dve.wait_ge(dec_done, 2)
                        for g in range(2):
                            last = V.tensor_tensor_scan(lb[:, g, :], la[:, g, :], xc[:, g, :], 0.0, ALU.mult, ALU.add)
                        chain(last)

                    def lru_out():
                        dve.wait_ge(gth_done, 1)
                        lg = T[:, T_LG:T_LG + 2, :]
                        chain(STT(ld[:, :, :], ld[:, :, :], 1.0, lg, ALU.add, ALU.mult))
                        STT(oT[:, 0:2, :], lb[:, :, :], 0.5, ld[:, :, :], ALU.mult, ALU.mult).then_inc(lru_done, 1)

                    def cmp_hidden():
                        dve.wait_ge(hgt_done, 1)
                        chain(STT(hg[:, 2, :, 0:N_CMP], hg[:, 1, :, 0:N_CMP], 1.0, hid[:, :, 0:N_CMP], ALU.add, ALU.mult))
                        V.tensor_copy(hrep[:, :, :, 0:N_CMP],
                                      hg[:, 2, 2:4, 0:N_CMP].unsqueeze(2).to_broadcast([P, 2, NSA_H, N_CMP])).then_inc(hrep_done, 1)

                    def cmp_softmax_in():
                        dve.wait_ge(aux_done, AUX["cmp_scores"] + 1)
                        v = lc[:, :, :, 0:N_CMP]
                        chain(TT(v, v, cmpm[:, 0, :, 0:N_CMP].unsqueeze(2).to_broadcast([P, NB, NSA_H, N_CMP]), ALU.add))
                        m8 = cst[:, 0, :].rearrange("p (b h) -> p b h", b=NB)
                        chain(V.tensor_reduce(m8, v, AX.X, ALU.max))
                        TT(v, v, m8.unsqueeze(3).to_broadcast([P, NB, NSA_H, N_CMP]), ALU.subtract).then_inc(lcd_done, 1)

                    def cmp_softmax_out():
                        dve.wait_ge(lce_done, 1)
                        v = pc[:, :, :, 0:N_CMP]
                        TT(v, lc[:, :, :, 0:N_CMP], cmpm[:, 1, :, 0:N_CMP].unsqueeze(2).to_broadcast([P, NB, NSA_H, N_CMP]),
                           ALU.mult).then_inc(pc_done, 1)
                        dve.wait_ge(pc_done, 1)
                        m8 = cst[:, 1, :].rearrange("p (b h) -> p b h", b=NB)
                        chain(V.tensor_reduce(m8, v, AX.X, ALU.add))
                        chain(TS(cst[:, 1, :], cst[:, 1, :], 1e-30, None, ALU.max))
                        chain(V.reciprocal(cst[:, 1, :], cst[:, 1, :]))
                        dve.wait_ge(ng_done, 1)
                        chain(TS(ng[:, :, :, :], ng[:, :, :, :], 1.0, 0.5, ALU.add, ALU.mult))
                        chain(TT(m8, m8, ng[:, :, :, 0], ALU.mult))

                    def cmp_out():
                        dve.wait_ge(aux_done, AUX["cmp_out"] + 1)
                        chain(TT(o_nsa[:, :, :, :].rearrange("p b h d -> p (b h) d"), oc[:, :, :, :].rearrange("p b h d -> p (b h) d"),
                                 cst[:, 1, :].unsqueeze(2).to_broadcast([P, NB * NSA_H, DH]), ALU.mult))

                    dn = nmax[:, FOX_H:SLC0, :].rearrange("p (g s) b -> p b g s", s=2)
                    dl = lsum[:, FOX_H:SLC0, :].rearrange("p (g s) b -> p b g s", s=2)

                    def d5(k):
                        return dst[:, k, :, :].rearrange("p b (g s) -> p b g s", s=2)

                    def dil_in():
                        m = cst[:, 2, 0:4].rearrange("p (b s) -> p b s", b=NB)
                        chain(TT(m, dn[:, :, 0, :], dn[:, :, 1, :], ALU.min))
                        chain(TT(m, m, dn[:, :, 2, :], ALU.min))
                        for g in range(3):
                            last = TT(d5(0)[:, :, g, :], m, dn[:, :, g, :], ALU.subtract)
                        last.then_inc(dw_in, 1)

                    def dil_out():
                        dve.wait_ge(dw_exp, 1)
                        w = d5(1)
                        for g in range(3):
                            last = TT(d5(2)[:, :, g, :], w[:, :, g, :], dl[:, :, g, :], ALU.mult)
                        chain(last)
                        s = cst[:, 3, 0:4].rearrange("p (b s) -> p b s", b=NB)
                        chain(TT(s, d5(2)[:, :, 0, :], d5(2)[:, :, 1, :], ALU.add))
                        chain(TT(s, s, d5(2)[:, :, 2, :], ALU.add))
                        chain(V.reciprocal(s, s))
                        for g in range(3):
                            last = TT(d5(3)[:, :, g, :], w[:, :, g, :], s, ALU.mult)
                        chain(last)
                        ov = o_dil[:, :, :, :]
                        for b in range(NB):
                            last = TT(ov[:, b, :, :], ov[:, b, :, :], dst[:, 3, b, :].unsqueeze(2).to_broadcast([P, DIL_H, DH]), ALU.mult)
                        chain(last)
                        chain(TT(o_dilm[:, :, :, :], ov[:, :, 0:2, :], ov[:, :, 2:4, :], ALU.add))
                        TT(o_dilm[:, :, :, :], o_dilm[:, :, :, :], ov[:, :, 4:6, :], ALU.add).then_inc(od_done, 1)

                    def merge(n):
                        (idx, b), half = BR_ORDER[n // 2], n % 2
                        g = (1, 0, 2, 3)[idx]
                        if n == 0:
                            dve.wait_ge(pmm_act, 2 * GCH)
                        dve.wait_ge(pmm_full, J_BR + n + 1)
                        m = merged[:, b, 512 * half:512 * half + 512]
                        STT(mtmp if idx else m, gate[:, b, g * D + 512 * half:g * D + 512 * half + 512], 1.0,
                            pmm[:, (J_BR + n) % 2, :], ALU.add, ALU.mult).then_inc(pmm_dve, 1)
                        if idx:
                            dve.wait_ge(pmm_dve, J_GATE + n + 1)
                            last = TT(m, m, mtmp, ALU.add)
                            if idx == 3 and half == 1:
                                last.then_inc(m_done, 1)
                                dve.wait_ge(m_done, b + 1)
                            else:
                                chain(last)

                    head_max(0)
                    for i in range(HEADS + 1):
                        if i + 1 < HEADS:
                            head_max(i + 1)
                        if i == HEADS:
                            merge(0)
                        if i >= 1:
                            take_out(i - 1)
                        if i < HEADS:
                            take_probsT(i)
                        if i == 0:
                            lru_root()
                        if i == 1:
                            cmp_hidden()
                        if i == 3:
                            lru_scan()
                        if i == 4:
                            lru_out()
                            cmp_softmax_in()
                        if i == 5:
                            cmp_softmax_out()
                        if i == 8:
                            cmp_out()
                        if i == 11:
                            dil_in()
                        if i == 13:
                            dil_out()

                    for n in range(1, 2 * len(BR_ORDER)):
                        merge(n)

                    def residual(b):
                        for half in range(2):
                            j = J_OUTS[2 * b + half]
                            dve.wait_ge(pmm_full, j + 1)
                            xs = x[:, b, 512 * half:512 * half + 512]
                            TT(xs, pmm[:, j % 2, :], xs, ALU.add).then_inc(pmm_dve, 1)
                        norm(NB, 1, (b,))

                    residual(0)

                    V.sem_inc(sums_done, RING)
                    V.sem_inc(es_used, 2)

                    LINKS_SUM = 5
                    count = [steps[0], 0]

                    def link(ins):
                        count[1] += 1
                        ins.then_inc(dve_step, 1)
                        dve.wait_ge(dve_step, count[0] + count[1])

                    def held():
                        dve.sem_inc(dve_held, 1)

                    def top(u, r, u_prev=None):
                        dve.wait_ge(es_full, u + 1)
                        s = [psc[:, r, a * P:(a + 1) * P] for a in range(PK)]
                        pairs = range(PK)

                        def both(f):
                            f(0)
                            return f(1)
                        held()
                        link(both(lambda a: V.max(tv[:, a, 0:8], s[a])))
                        held()
                        both(lambda a: V.max_index(ti[:, a, 0:8], tv[:, a, 0:8], s[a]))
                        last = both(lambda a: V.match_replace(srest[:, a, :], tv[:, a, 0:8], s[a], -3.0e38))
                        last.then_inc(es_used, 1)
                        dve.wait_ge(es_used, u + 3)
                        held()
                        link(both(lambda a: V.max(tv[:, a, 8:16], srest[:, a, :])))
                        held()
                        link(both(lambda a: V.max_index(ti[:, a, 8:16], tv[:, a, 8:16], srest[:, a, :])))
                        TS(tif[:, 0, :], ti[:, 0, :], float(N_KEYS), loff[:, 0:1], ALU.mult, ALU.add)
                        V.tensor_copy(tif[:, 1, :], ti[:, 1, :])
                        link(TT(cand[:, :, :], tv[:, 0, :].unsqueeze(2).to_broadcast([P, 16, 16]),
                                tv[:, 1, :].unsqueeze(1).to_broadcast([P, 16, 16]), ALU.add))
                        cf = cand[:, :, :].rearrange("p i j -> p (i j)")
                        held()
                        link(V.max(cv[:, 0:8], cf))
                        held()
                        V.max_index(cpos[:, 0:8], cv[:, 0:8], cf)
                        link(V.match_replace(crest[:, :], cv[:, 0:8], cf, -3.0e38))
                        held()
                        link(V.max(cv[:, 8:16], crest[:, :]))
                        held()
                        link(V.max_index(cpos[:, 8:16], cv[:, 8:16], crest[:, :]))
                        TS(cij[:, 0, :], cpos[:, :], 4, None, ALU.logical_shift_right)
                        link(TS(cij[:, 1, :], cpos[:, :], 15, None, ALU.bitwise_and))
                        link(V.tensor_copy(cijf[:, :, :], cij[:, :, :]))
                        f3 = onehot[:, :, :, :].rearrange("p a k j -> p (a k) j")
                        link(TT(f3, cijf[:, :, :].rearrange("p a k -> p (a k)").unsqueeze(2).to_broadcast([P, 32, 16]),
                                iota16[:, :].unsqueeze(1).to_broadcast([P, 32, 16]), ALU.is_equal))
                        link(TT(onehot[:, :, :, :], onehot[:, :, :, :], tif[:, :, :].unsqueeze(2).to_broadcast([P, 2, 16, 16]), ALU.mult))
                        link(V.tensor_reduce(eij[:, :, :].rearrange("p a k -> p (a k)"), f3, AX.X, ALU.add))
                        TS(sdiff[:, r, :], cv[:, :], cv[:, 0:1], None, ALU.subtract)
                        if u_prev is not None:
                            dve.wait_ge(idx_taken, u_prev + 1)
                        TT(eidx[:, r, :], eij[:, 0, :], eij[:, 1, :], ALU.add).then_inc(top_done, 1)

                    def dots(u, r):
                        h_ps = ppo[:, :, :].rearrange("p a c -> p (a c)")
                        for k in range(TOPK):
                            dve.wait_ge(row_landed[k], (l * UNITS + u) * 32 + 16)
                            V.tensor_tensor_reduce(out=junk[:, :], in0=rows[:, k, :], in1=h_ps, scale=1.0, scalar=0.0,
                                                   op0=ALU.mult, op1=ALU.add,
                                                   accum_out=actv[:, k:k + 1]).then_inc(dots_done, 1)
                            dve.wait_ge(dots_done, u * TOPK + k + 1)
                        link(TT(ga[:, 0, :], actv[:, :], actv[:, :], ALU.mult))
                        link(TS(ga[:, 1, :], ga[:, 0, :], GELU_C, 1.0, ALU.mult, ALU.add))
                        TT(gin[:, r, :], ga[:, 1, :], actv[:, :], ALU.mult).then_inc(gin2_done, 1)
                        dve.wait_ge(sexp_done, u + 1)
                        link(V.reciprocal(srl[:, :], sl[:, r, :]))
                        link(TS(gw[:, :], sexp[:, r, :], srl[:, 0:1], 0.5, ALU.mult, ALU.mult))
                        dve.wait_ge(gt2_done, u + 1)
                        link(STT(ga[:, 0, :], gt[:, r, :], 1.0, actv[:, :], ALU.add, ALU.mult))
                        TT(wv[:, r, :], ga[:, 0, :], gw[:, :], ALU.mult).then_inc(w_ready, 1)

                    top(0, 0)
                    links_top = count[1]
                    steps[0] = count[0] + count[1]
                    residual(1)
                    count[0], count[1] = steps[0], 0
                    dve.wait_ge(pe_in, 1)
                    dots(0, 0)
                    top(1, 1)
                    top(2, 0, 0)
                    dots(1, 1)
                    top(3, 1, 1)
                    links_pair = 2 * (links_top + LINKS_SUM)
                    start = count[0] + count[1] - links_pair

                    def pair(p, more):
                        count[0], count[1] = p * links_pair + start, 0
                        for r in range(2):
                            dots(2 * p + r, r)
                            if more:
                                top(2 * p + r + 2, r, 2 * p + r)
                        assert not more or count[1] == links_pair

                    with dve.Fori(1, UNITS // 4) as p:
                        pair(p, True)
                    dve.wait_ge(pe_in, 2)
                    with dve.Fori(UNITS // 4, UNITS // 2 - 1) as p:
                        pair(p, True)
                    pair(UNITS // 2 - 1, False)
                    dve.wait_ge(w_ready, UNITS)
                    rest = h[:, 1, :]
                    for k in range(PE_SHARE, TOPK):
                        dve.wait_ge(row_landed[k], (l * UNITS + UNITS - 1) * 32 + 32)
                        w = wv[:, 1, k:k + 1]
                        if k == PE_SHARE:
                            link(TS(rest, rows[:, k, :], w, None, ALU.mult))
                        else:
                            link(STT(rest, rows[:, k, :], w, rest, ALU.mult, ALU.add))
                    dve.wait_ge(sums_done, UNITS * TOPK - (TOPK - PE_SHARE) + RING)
                    TT(x[:, 1, :], paux[:, :, :].rearrange("p a c -> p (a c)"), rest, ALU.add)
                    TS(loff[:, :], loff[:, :], float(N_EXPERTS), None, ALU.add)

            numbers = [s.num for s in sems]
            assert numbers == list(range(numbers[0], numbers[-1] + 1))
            nc.sync.sem_clear(range(numbers[0], numbers[-1] + 1))
            nc.all_engine_barrier()

        with nc.Block() as block:
            @block.sync
            def _(sp):
                for b in range(NB):
                    sp.wait_ge(s_out, 1 + b)
                    sp.dma_start(out[0].rearrange("(b p) d -> p b d", p=P)[:, b, :], h[:, b, :]).then_inc(s_stored, 16)
                sp.wait_ge(s_stored, 16 * NB)

            @block.scalar
            def _(act):
                for b in range(NB):
                    nc.scalar.activation(junk[:, :], x[:, b, :], ACT.Square, accum_out=stat[:, b:b + 1]).then_inc(s_std, 1)
                    act.wait_ge(s_std, 2 * b + 1)
                    nc.scalar.activation(stat[:, 2 + b:3 + b], stat[:, b:b + 1], ACT.Sqrt, bias=eps[:, :],
                                         scale=1.0 / D).then_inc(s_std, 1)

            @block.vector
            def _(dve):
                for b in range(NB):
                    dve.wait_ge(s_std, 2 * b + 2)
                    nc.vector.reciprocal(stat[:, 4 + b:5 + b], stat[:, 2 + b:3 + b]).then_inc(s_rec, 1)
                    dve.wait_ge(s_rec, b + 1)
                    nc.vector.scalar_tensor_tensor(h[:, b, :], x[:, b, :], stat[:, 4 + b:5 + b], gain,
                                                   ALU.mult, ALU.mult).then_inc(s_out, 1)


_INS = ['x', 'gains', 'w_in', 'fox_b_f', 'lru_conv_w', 'lru_conv_b', 'lru_w_a', 'lru_b_a',
        'lru_w_x', 'lru_b_x', 'lru_lambda', 'nsa_pe_k', 'nsa_pe_v', 'nsa_w1_k', 'nsa_w2_k',
        'nsa_w1_v', 'nsa_w2_v', 'w_br_fox', 'w_br_lru', 'w_br_dil', 'w_br_nsa', 'w_out',
        'norm2_g', 'peer_w_q', 'peer_sub_keys', 'peer_u', 'peer_v']


def _constants(np):
    f = np.float32
    pos = np.arange(256, dtype=f)
    freqs = (f(10000.0) ** (-np.arange(32, dtype=f) / f(32))).astype(f)
    ang = (pos[:, None] * freqs[None, :]).astype(f)
    cos, sin = np.cos(ang).astype(f), np.sin(ang).astype(f)
    rope = np.stack([np.concatenate([cos, cos], 1), np.concatenate([-sin, sin], 1)], 1)
    rope = rope.reshape(2, 128, 2, 64).transpose(1, 0, 2, 3).reshape(128, 256)
    q = np.arange(128)
    masks = np.zeros((128, 4, 384), f)
    for b in range(2):
        dist = (b * 128 + q)[:, None] - np.arange((b + 1) * 128)[None, :]
        ok = [dist >= 0, (dist >= 0) & (dist <= 128), (dist >= 0) & (dist % 4 == 0), (dist >= 0) & (dist % 16 == 0)]
        for m in range(4):
            masks[:, m, 128 * b:128 * b + (b + 1) * 128] = np.where(ok[m], 0.0, NEG)
    end = 16 * np.arange(16) + 31
    ok = end[None, None, :] <= (np.arange(2)[None, :, None] * 128 + q[:, None, None])
    cmp = np.stack([np.where(ok, 0.0, NEG), np.where(ok, 1.0, 0.0)], 1).astype(f)
    pick = np.zeros((4, 2, 4, 128), f)
    for h in range(4):
        pick[h, 0, h] = 1.0
        pick[h, 1, h] = -1.0
    return {"c_ident": np.eye(128, dtype=f), "c_rope": np.ascontiguousarray(rope),
            "c_masks": masks.reshape(128, -1), "c_cmp": cmp.reshape(128, -1), "c_pick": pick.reshape(4, -1)}


def kernel(**inputs):
    import numpy as _np
    import concourse.bacc as _bacc
    from concourse import mybir as _mybir
    from concourse.bass_utils import run_bass_kernel_spmd as _run

    nc = _bacc.Bacc("TRN2", target_bir_lowering=False, num_devices=1)
    arrays, args = {}, []
    inputs["gains"] = _np.concatenate([inputs["norm1_g"], inputs["final_g"][None]])
    for name, a in [(n, inputs[n]) for n in _INS] + list(_constants(_np).items()):
        a = _np.ascontiguousarray(a)
        arrays[f"in_{name}_dram"] = a
        args.append(nc.dram_tensor(f"in_{name}_dram", a.shape, _mybir.dt.from_np(a.dtype), kind="ExternalInput").ap())
    args.append(nc.dram_tensor("out_0_dram", (1, SEQ, D), _mybir.dt.float32, kind="ExternalOutput").ap())
    hybrid_decoder(nc, *args)
    r = _run(nc, [arrays], core_ids=[0])
    return r.results[0]["out_0_dram"]
```
